# Optimizing a Trainium2 kernel written in Bass

```python
import math
import jax, jax.numpy as jnp
from jax import lax
import numpy as np

D_MODEL = 1024
BATCH = 1
SEQ = 1024
DEPTH = 1

N_HEADS = 16
HEAD_DIM = 64
MIX_WIDTH = N_HEADS * HEAD_DIM
N_MIXERS = 2
SB_Q_BLOCK = 128
MOBA_BLOCK = 256
MOBA_TOPK = 3
MOBA_Q_CHUNK = 32
REL_BUCKETS = 32
REL_MAX_DIST = 128
LN_EPS = 1e-5
DEEPNORM_ALPHA = (2.0 * DEPTH) ** 0.25
DEEPNORM_BETA = (8.0 * DEPTH) ** -0.25
NEG_INF = -1e30

kernel_name = "hybrid_stickbreak_moba_deepnorm"

def layer_norm(x, g, b):
    xf = x.astype(jnp.float32)
    mu = jnp.mean(xf, axis=-1, keepdims=True)
    var = jnp.mean(jnp.square(xf - mu), axis=-1, keepdims=True)
    y = (xf - mu) * lax.rsqrt(var + LN_EPS) * g.astype(jnp.float32) + b.astype(jnp.float32)
    return y.astype(x.dtype)

def t5_bucket(dist):
    n = jnp.maximum(dist, 0)
    max_exact = REL_BUCKETS // 2
    nf = jnp.maximum(n, 1).astype(jnp.float32)
    large = max_exact + (jnp.log(nf / max_exact) / math.log(REL_MAX_DIST / max_exact)
                         * (REL_BUCKETS - max_exact)).astype(jnp.int32)
    large = jnp.minimum(large, REL_BUCKETS - 1)
    return jnp.where(n < max_exact, n, large)

def split_heads(t):
    B, S, _ = t.shape
    return t.reshape(B, S, N_HEADS, HEAD_DIM).transpose(0, 2, 1, 3)

def stick_breaking_attention(q, k, v):
    S = q.shape[2]
    scale = HEAD_DIM ** -0.5
    outs = []
    for blk in range(S // SB_Q_BLOCK):
        q0 = blk * SB_Q_BLOCK
        q1 = q0 + SB_Q_BLOCK
        qb = q[:, :, q0:q1]
        kb = k[:, :, :q1]
        vb = v[:, :, :q1]
        z = jnp.einsum('bhqd,bhkd->bhqk', qb, kb).astype(jnp.float32) * scale
        past = jnp.arange(q1)[None, :] < jnp.arange(q0, q1)[:, None]
        log_1mb = jnp.where(past, jax.nn.log_sigmoid(-z), 0.0)
        rev_cs = lax.cumsum(log_1mb, axis=log_1mb.ndim - 1, reverse=True)
        log_w = jax.nn.log_sigmoid(z) + rev_cs - log_1mb
        w = jnp.where(past, jnp.exp(log_w), 0.0)
        outs.append(jnp.einsum('bhqk,bhkd->bhqd', w.astype(v.dtype), vb))
    return jnp.concatenate(outs, axis=2)

def moba_attention(q, k, v, rel_table):
    B, H, S, Dh = q.shape
    scale = Dh ** -0.5
    nb = -(-S // MOBA_BLOCK)
    pad = nb * MOBA_BLOCK - S
    kp = jnp.pad(k, ((0, 0), (0, 0), (0, pad), (0, 0)))
    vp = jnp.pad(v, ((0, 0), (0, 0), (0, pad), (0, 0)))
    k_blocks = kp.reshape(B, H, nb, MOBA_BLOCK, Dh)
    v_blocks = vp.reshape(B, H, nb, MOBA_BLOCK, Dh)
    k_mean = jnp.mean(k_blocks.astype(jnp.float32), axis=3)

    pos = jnp.arange(S, dtype=jnp.int32)
    own = pos // MOBA_BLOCK
    gate = jnp.einsum('bhsd,bhnd->bhsn', q.astype(jnp.float32), k_mean)
    past_block = jnp.arange(nb)[None, :] < own[:, None]
    gate = jnp.where(past_block, gate, NEG_INF)
    kk = min(MOBA_TOPK, nb)
    _, top_idx = lax.top_k(gate, kk)
    top_ok = jnp.arange(kk)[None, :] < jnp.minimum(own, MOBA_TOPK)[:, None]
    own_idx = jnp.broadcast_to(own[None, None, :, None], (B, H, S, 1))
    sel_idx = jnp.concatenate([top_idx.astype(jnp.int32), own_idx], axis=-1)
    slot_ok = jnp.concatenate([top_ok, jnp.ones((S, 1), dtype=bool)], axis=-1)
    J = kk + 1

    nc = S // MOBA_Q_CHUNK
    C = MOBA_Q_CHUNK
    q_c = jnp.moveaxis(q.reshape(B, H, nc, C, Dh), 2, 0)
    idx_c = jnp.moveaxis(sel_idx.reshape(B, H, nc, C, J), 2, 0)
    ok_c = slot_ok.reshape(nc, C, J)
    qpos_c = pos.reshape(nc, C)
    bi = jnp.arange(B)[:, None, None, None]
    hi = jnp.arange(H)[None, :, None, None]
    hi5 = jnp.arange(H)[None, :, None, None, None]
    offs = jnp.arange(MOBA_BLOCK, dtype=jnp.int32)

    def chunk_fn(args):
        qc, idxc, okc, qposc = args
        kg = k_blocks[bi, hi, idxc]
        vg = v_blocks[bi, hi, idxc]
        kpos = idxc[..., None] * MOBA_BLOCK + offs
        dist = qposc[None, None, :, None, None] - kpos
        valid = okc[None, None, :, :, None] & (dist >= 0)
        bias = rel_table[t5_bucket(dist), hi5].astype(jnp.float32)
        logits = jnp.einsum('bhcd,bhcjld->bhcjl', qc, kg).astype(jnp.float32) * scale + bias
        logits = jnp.where(valid, logits, NEG_INF).reshape(B, H, C, J * MOBA_BLOCK)
        p = jax.nn.softmax(logits, axis=-1).reshape(B, H, C, J, MOBA_BLOCK)
        return jnp.einsum('bhcjl,bhcjld->bhcd', p.astype(vg.dtype), vg)

    out = lax.map(chunk_fn, (q_c, idx_c, ok_c, qpos_c))
    return jnp.moveaxis(out, 0, 2).reshape(B, H, S, Dh)

def hybrid_layer(x, w_in, w_out, ln_g, ln_b, rel_table, mixer_id):
    B, S, _ = x.shape
    proj = jnp.einsum('bsd,de->bse', x, w_in)
    q, k, v, g = jnp.split(proj, 4, axis=-1)
    q, k, v = split_heads(q), split_heads(k), split_heads(v)
    if mixer_id == 0:
        o = stick_breaking_attention(q, k, v)
    else:
        o = moba_attention(q, k, v, rel_table)
    o = o.transpose(0, 2, 1, 3).reshape(B, S, MIX_WIDTH)
    y = jnp.einsum('bse,ed->bsd', o * jax.nn.silu(g), w_out)
    return layer_norm(DEEPNORM_ALPHA * x + y, ln_g, ln_b)

def setup_inputs(seed: int = 0) -> dict:
    key = jax.random.key(seed)
    kx, kin, kout, kg, kb, kr = jax.random.split(key, 6)
    x = jax.random.normal(kx, (BATCH, SEQ, D_MODEL), jnp.float32)
    w_in = jax.random.normal(kin, (DEPTH, D_MODEL, 4 * MIX_WIDTH), jnp.float32) * D_MODEL ** -0.5
    w_out = (jax.random.normal(kout, (DEPTH, MIX_WIDTH, D_MODEL), jnp.float32)
             * MIX_WIDTH ** -0.5 * DEEPNORM_BETA)
    ln_g = 1.0 + 0.02 * jax.random.normal(kg, (DEPTH, D_MODEL), jnp.float32)
    ln_b = 0.02 * jax.random.normal(kb, (DEPTH, D_MODEL), jnp.float32)
    rel_table = 0.2 * jax.random.normal(kr, (REL_BUCKETS, N_HEADS), jnp.float32)
    return {"x": x, "w_in": w_in, "w_out": w_out, "ln_g": ln_g, "ln_b": ln_b,
            "rel_table": rel_table}

def reference(x, w_in, w_out, ln_g, ln_b, rel_table):
    h = x
    for layer in range(DEPTH):
        h = hybrid_layer(h, w_in[layer], w_out[layer], ln_g[layer], ln_b[layer],
                         rel_table, layer % N_MIXERS)
    return h


_drawn_inputs = setup_inputs


def setup_inputs(seed=0):
    import zlib

    import numpy as np

    out = dict(_drawn_inputs(seed))
    spreads = {}
    factors = {}
    for name, (base, spread) in spreads.items():
        noise = np.random.default_rng([zlib.crc32(name.encode()), seed]).standard_normal(out[name].shape)
        drawn = base * np.exp(spread * noise) if base else spread * noise
        out[name] = __import__('jax').numpy.asarray(drawn.astype(out[name].dtype))
    for name, factor in factors.items():
        out[name] = (out[name] * factor).astype(out[name].dtype)
    return out
```

```python
from contextlib import ExitStack

import concourse.bass as bass
from concourse import mybir

F32 = mybir.dt.float32
F32R = mybir.dt.float32r
BF16 = mybir.dt.bfloat16
ALU = mybir.AluOpType
ACT = mybir.ActivationFunctionType

P = 128
SEQ = 1024
DM = 1024
HEAD = 64
PAIRS = 8
KT = DM // P
ST = SEQ // P
HALF = SEQ // 2
QH = ST // 2
SCALE = float(HEAD) ** -0.5
ALPHA = 2.0 ** 0.25
EPS = 1e-5
MASKED = -1e30

K_, Q_, V_, G_ = range(4)
HALVES = {K_: (0, 1), Q_: (0, 1), V_: (1, 0), G_: (0, 1)}

PROJ = (0, 1)
ZB = (2, 3, 4)
TB = (5, 6)
OB = 7

CHUNKS = 24
TILES = 16
STEPS = 24
TRANS = 2 + STEPS

UNITS = [(0, 0), (0, 1), (1, 0), (1, 1)]
CHUNK0 = [0, 8, 12, 20]
TILE0 = [0, 4, 8, 12]
STEP0 = [0, 8, 12, 20]


def chunks_of(tile):
    first = P * tile
    keys = SEQ - first
    return [(first, min(keys, HALF))] + ([(first + HALF, keys - HALF)] if keys > HALF else [])


CHUNK_LIST = [(u, half * QH + i, c) for u, (_, half) in enumerate(UNITS) for i in range(QH)
              for c in range(len(chunks_of(half * QH + i)))]


def w_offset(tile):
    half = tile // QH
    return sum(SEQ - P * t for t in range(half * QH, tile))


W_SIZE = [w_offset(QH - 1) + SEQ - P * (QH - 1), w_offset(ST - 1) + SEQ - P * (ST - 1)]


def key_tiles(unit):
    return list(range(ST - 1, UNITS[unit][1] * QH - 1, -1))


def stick_breaking_layer(nc, xT, x_rows, w_in, w_out, ln_g, ln_b, consts_f, consts_b, out):
    with ExitStack() as ctx:
        def sb(name, shape, dt=F32):
            return ctx.enter_context(nc.sbuf_tensor(name, shape, dt))

        def sem(name):
            return ctx.enter_context(nc.semaphore(name))

        ps = ctx.enter_context(nc.psum_tensor("ps", [P, 8, HALF], F32))

        x_hi = sb("x_hi", [P, KT, SEQ], F32R)
        x_lo = sb("x_lo", [P, KT, SEQ], F32R)
        w_raw = sb("w_raw", [P, 4, KT * P])
        w_hi = sb("w_hi", [P, 2, KT * P], F32R)
        w_lo = sb("w_lo", [P, 2, KT * P], F32R)
        kk = sb("kk", [P, 4, SEQ], F32R)
        qq = sb("qq", [P, 2, SEQ], F32R)
        vT = sb("vT", [P, SEQ])
        vv = sb("vv", [P, ST, 2, 2 * HEAD], F32R)
        gated = sb("gated", [P, PAIRS, SEQ])
        silu = sb("silu", [P, SEQ])
        take = [sb(f"take{h}", [P, W_SIZE[h]]) for h in range(2)]
        keep = sb("keep", [P, 2, SEQ])
        wt_hi = sb("wt_hi", [P, 2, HALF], F32R)
        wt_lo = sb("wt_lo", [P, 2, HALF], F32R)
        osum = sb("osum", [P, 2, HALF])
        ident = sb("ident", [P, P])
        ident_b = sb("ident_b", [P, 2, P], BF16)
        ones = sb("ones", [P, 1])
        stats = sb("stats", [P, 2, 2, 6])
        moments = sb("moments", [P, 2, 8])

        x_loaded = [sem(f"x_loaded{k}") for k in range(KT)]
        consts_loaded = sem("consts_loaded")
        w_loaded = [sem(f"w_loaded{o}") for o in range(4)]
        k_copied = sem("k_copied")
        ones_set = sem("ones_set")
        x_hi_done = sem("x_hi_done")
        x_lo_done = sem("x_lo_done")
        w_hi_done = sem("w_hi_done")
        w_split = sem("w_split")
        projected = sem("projected")
        proj_hi_done = sem("proj_hi_done")
        bank_free = [sem("bank_free0"), sem("bank_free1")]
        z_done = sem("z_done")
        sigmoids_done = sem("sigmoids_done")
        scanned = sem("scanned")
        w_ready = sem("w_ready")
        transposed = sem("transposed")
        t_hi_done = sem("t_hi_done")
        t_split = sem("t_split")
        stepped = sem("stepped")
        o_moved = sem("o_moved")
        o_summed = sem("o_summed")
        gated_done = sem("gated_done")
        wo_loaded = [sem(f"wo_loaded{r}") for r in range(2)]
        wo_hi_done = sem("wo_hi_done")
        wo_split = sem("wo_split")
        gs_hi_done = sem("gs_hi_done")
        gs_split = sem("gs_split")
        lnp_loaded = sem("lnp_loaded")
        res_loaded = [sem("res_loaded0"), sem("res_loaded1")]
        y_done = sem("y_done")
        ln_step = sem("ln_step")
        root_done = sem("root_done")
        y_read = sem("y_read")
        scaled = sem("scaled")
        normed = sem("normed")
        stored = [sem("stored0"), sem("stored1")]

        wo_hi, wo_lo = x_hi, x_lo
        gs = kk
        ln_par = keep
        take0 = take[0][:, 0:3 * DM].rearrange("p (n d) -> p n d", n=3)
        res = [take0[:, 0, :], take0[:, 1, :]]
        yt = [take0[:, 2, :], vT[:, :]]
        root = moments

        block = ctx.enter_context(nc.Block())

        @block.sync
        def _(sp):
            def load_w(p, o):
                sp.dma_start(w_raw[:, o, :], w_in[p, o]).then_inc(w_loaded[o], 16)

            sp.dma_start(gated[:, 0, :], xT[0]).then_inc(x_loaded[0], 16)
            load_w(0, K_)
            for k in range(1, KT):
                sp.dma_start(gated[:, k, :], xT[k]).then_inc(x_loaded[k], 16)
            load_w(0, Q_)
            sp.dma_start(ident[:, :], consts_f).then_inc(consts_loaded, 16)
            sp.dma_start(ident_b[:, :, :], consts_b).then_inc(consts_loaded, 16)
            load_w(0, V_)
            load_w(0, G_)

            def duplicate_k(p):
                for h in range(2):
                    sp.wait_ge(bank_free[h], 4 * p + K_ + 1)
                sp.dma_start(kk[HEAD:P, 0:2, :].bitcast(F32), kk[0:HEAD, 0:2, :].bitcast(F32)).then_inc(k_copied, 16)
                sp.dma_start(kk[0:HEAD, 2:4, :].bitcast(F32), kk[HEAD:P, 2:4, :].bitcast(F32)).then_inc(k_copied, 16)

            def body(p):
                for o in (K_, Q_, V_, G_):
                    sp.wait_ge(w_split, 4 * p + o + 1)
                    load_w(p + 1, o)
                duplicate_k(p + 1)

            duplicate_k(0)
            body(0)
            with sp.Fori(1, PAIRS - 1) as p:
                body(p)

            for r in range(2):
                if r == 0:
                    sp.wait_ge(w_split, 4 * PAIRS)
                else:
                    sp.wait_ge(wo_split, 4)
                sp.dma_start(w_raw[:, :, :], w_out[r]).then_inc(wo_loaded[r], 16)
            sp.wait_ge(w_ready, TILES * PAIRS)
            sp.dma_start(ln_par[:, 0, :], ln_g.broadcast_to([P, DM])).then_inc(lnp_loaded, 16)
            sp.dma_start(ln_par[:, 1, :], ln_b.broadcast_to([P, DM])).then_inc(lnp_loaded, 16)
            sp.wait_ge(transposed, TRANS * (PAIRS - 1) + 2 + STEP0[3])
            for s in range(2):
                sp.dma_start(res[s], x_rows[s]).then_inc(res_loaded[s], 16)
            for s in range(ST):
                sp.wait_ge(normed, s + 1)
                sp.dma_start(out[s], res[s % 2]).then_inc(stored[s % 2], 16)
                if s + 2 < ST:
                    sp.wait_ge(stored[s % 2], 16 * (s // 2 + 1))
                    sp.dma_start(res[s % 2], x_rows[s + 2]).then_inc(res_loaded[s % 2], 16)
            for b in range(2):
                sp.wait_ge(stored[b], 16 * (ST // 2))

        @block.tensor
        def _(pe):
            def project(p, o, first, count):
                for m in range(first, first + count):
                    n, k, part = m // (3 * KT), m // 3 % KT, m % 3
                    h = HALVES[o][n]
                    if m == 0:
                        pe.wait_ge(w_split, 4 * p + o + 1)
                    if m % (3 * KT) == 0 and not (o == K_ and isinstance(p, int) and p == 0):
                        pe.wait_ge(bank_free[h], 4 * p + o)
                    if o == K_ and isinstance(p, int) and p == 0 and part == 0 and n == 0:
                        pe.wait_ge(x_lo_done, k + 1)
                    slot = o % 2
                    w = (w_hi, w_hi, w_lo)[part][:, slot, k * P:(k + 1) * P]
                    x = (x_hi, x_lo, x_hi)[part][:, k, h * HALF:(h + 1) * HALF]
                    mm = nc.tensor.matmul(ps[:, PROJ[h], :], w, x, start=(m % (3 * KT) == 0),
                                          stop=(m % (3 * KT) == 3 * KT - 1))
                    if m % (3 * KT) == 3 * KT - 1:
                        mm.then_inc(projected, 1)

            def scores(p, n):
                unit, tile, c = CHUNK_LIST[n]
                head = UNITS[unit][0]
                key, keys = chunks_of(tile)[c]
                if n in (0, CHUNK0[2]):
                    pe.wait_ge(k_copied, 32 * (p + 1))
                    for h in range(2):
                        pe.wait_ge(bank_free[h], 4 * p + Q_ + 1)
                if n >= len(ZB) or not (isinstance(p, int) and p == 0):
                    pe.wait_ge(sigmoids_done, CHUNKS * p + n - len(ZB) + 1)
                z = ps[:, ZB[n % len(ZB)], 0:keys]
                q = qq[:, head, tile * P:(tile + 1) * P]
                nc.tensor.matmul(z, q, kk[:, 2 * head, key:key + keys], start=True, stop=False)
                if c == 0:
                    nc.tensor.matmul(z[:, 0:P], ident_b[:, 0, :], ident_b[:, 1, :], start=False, stop=False)
                nc.tensor.matmul(z, q, kk[:, 2 * head + 1, key:key + keys], start=False,
                                 stop=True).then_inc(z_done, 1)

            def transpose_v(p, n):
                h = HALVES[V_][n]
                pe.wait_ge(bank_free[h], 4 * p + V_ + 1)
                if not (isinstance(p, int) and p == 0):
                    pe.wait_ge(t_split, TRANS * p + n - 1)
                for i in range(QH):
                    t = h * QH + i
                    mm = nc.tensor.transpose(ps[:, TB[n % 2], i * P:(i + 1) * P], vT[:, t * P:(t + 1) * P],
                                             ident[:, :])
                mm.then_inc(transposed, 1)

            def transpose_w(p, unit, j):
                head, half = UNITS[unit]
                tile = key_tiles(unit)[j]
                if j == 0:
                    pe.wait_ge(w_ready, TILES * p + TILE0[unit] + QH)
                n = STEP0[unit] + j
                pe.wait_ge(t_split, TRANS * p + 2 + n - 1)
                for i in range(min(tile - half * QH + 1, QH)):
                    q = half * QH + i
                    at = w_offset(q) + (tile - q) * P
                    mm = nc.tensor.transpose(ps[:, TB[n % 2], i * P:(i + 1) * P], take[half][:, at:at + P],
                                             ident[:, :])
                mm.then_inc(transposed, 1)

            def values(p, unit, j):
                head, half = UNITS[unit]
                tile = key_tiles(unit)[j]
                n = STEP0[unit] + j
                pe.wait_ge(t_split, TRANS * p + 2 + n + 1)
                if j == 0 and not (unit == 0 and isinstance(p, int) and p == 0):
                    pe.wait_ge(o_summed, 4 * p + unit)
                cols = min(tile - half * QH + 1, QH) * P
                last = j == len(key_tiles(unit)) - 1
                nc.tensor.matmul(ps[:, OB, 0:cols], vv[:, tile, head, :], wt_hi[:, n % 2, 0:cols],
                                 start=(j == 0), stop=False)
                nc.tensor.matmul(ps[:, OB, 0:cols], vv[:, tile, head, :], wt_lo[:, n % 2, 0:cols],
                                 start=False, stop=last).then_inc(stepped, 1)

            def last_unit_tail(p, fill):
                for j in range(4):
                    transpose_w(p, 3, j)
                    fill(j)
                    if j:
                        values(p, 3, j - 1)
                values(p, 3, 3)

            def body(p, first=False, last=False):
                if first:
                    project(p, V_, 0, 32)
                else:
                    last_unit_tail(p - 1, lambda j: project(p, V_, 8 * j, 8))
                for s in range(4):
                    scores(p, 2 * s)
                    project(p, V_, 32 + 4 * s, 2)
                    scores(p, 2 * s + 1)
                    project(p, V_, 34 + 4 * s, 2)
                    if s == 1:
                        transpose_v(p, 0)
                project(p, G_, 0, 8)
                transpose_v(p, 1)
                for j in range(8):
                    transpose_w(p, 0, j)
                    if j < 4:
                        scores(p, CHUNK0[1] + j)
                    project(p, G_, 8 + 5 * j, 5)
                    if j:
                        values(p, 0, j - 1)
                for j in range(4):
                    transpose_w(p, 1, j)
                    if j == 0:
                        values(p, 0, 7)
                    else:
                        values(p, 1, j - 1)
                    scores(p, CHUNK0[2] + 2 * j)
                    if not last:
                        project(p + 1, K_, 12 * j, 6)
                    scores(p, CHUNK0[2] + 2 * j + 1)
                    if not last:
                        project(p + 1, K_, 12 * j + 6, 6)
                for j in range(8):
                    if j < 2:
                        scores(p, CHUNK0[3] + 2 * j)
                    transpose_w(p, 2, j)
                    if j == 0:
                        values(p, 1, 3)
                    else:
                        values(p, 2, j - 1)
                    if j < 2:
                        scores(p, CHUNK0[3] + 2 * j + 1)
                    elif not last:
                        project(p + 1, Q_, 8 * (j - 2), 8)
                values(p, 2, 7)

            project(0, K_, 0, 48)
            project(0, Q_, 0, 48)
            pe.wait_ge(consts_loaded, 32)
            body(0, first=True)
            with pe.Fori(1, PAIRS - 1) as p:
                body(p)
            body(PAIRS - 1, last=True)
            last_unit_tail(PAIRS - 1, lambda j: None)

            for s in range(ST):
                y = ps[:, 2 * (s % 2):2 * (s % 2) + 2, :]
                pe.wait_ge(gs_split, s + 1)
                if s == 0:
                    pe.wait_ge(sigmoids_done, CHUNKS * PAIRS)
                    for h in range(2):
                        pe.wait_ge(bank_free[h], 4 * PAIRS)
                if s >= 2:
                    pe.wait_ge(y_read, s - 1)
                for h in range(2):
                    for e in range(PAIRS):
                        if s == 0 and h == 0:
                            pe.wait_ge(wo_split, e + 1)
                        for part in range(3):
                            a = gs[:, 2 * (s % 2) + (0, 0, 1)[part], e * P:(e + 1) * P]
                            b = (wo_hi, wo_lo, wo_hi)[part][:, e, h * HALF:(h + 1) * HALF]
                            mm = nc.tensor.matmul(y[:, h, :], a, b, start=(e == 0 and part == 0),
                                                  stop=(e == PAIRS - 1 and part == 2))
                mm.then_inc(y_done, 1)

        @block.scalar
        def _(act):
            def copy(dst, src):
                return nc.scalar.activation(dst, src, ACT.Copy)

            def sigmoids(p, n):
                unit, tile, c = CHUNK_LIST[n]
                half = UNITS[unit][1]
                key, keys = chunks_of(tile)[c]
                number = TILE0[unit] + tile - half * QH
                act.wait_ge(z_done, CHUNKS * p + n + 1)
                if c == 0 and (number >= 2 or not (isinstance(p, int) and p == 0)):
                    act.wait_ge(w_ready, TILES * p + number - 1)
                if n == CHUNK0[unit] and (unit >= 2 or not (isinstance(p, int) and p == 0)):
                    before = STEP0[unit - 1] if unit >= 2 else STEP0[unit + 2] + (8, 4)[half] - TRANS
                    act.wait_ge(transposed, TRANS * p + 2 + before)
                z = ps[:, ZB[n % len(ZB)], 0:keys]
                off = key - P * tile
                nc.scalar.activation(keep[:, number % 2, off:off + keys], z, ACT.Sigmoid, scale=-SCALE)
                at = w_offset(tile) + off
                nc.scalar.activation(take[half][:, at:at + keys], z, ACT.Sigmoid,
                                     scale=SCALE).then_inc(sigmoids_done, 1)

            def wt_high(p, unit, j):
                n = STEP0[unit] + j
                cols = min(key_tiles(unit)[j] - UNITS[unit][1] * QH + 1, QH) * P
                act.wait_ge(transposed, TRANS * p + 2 + n + 1)
                if n >= 2 or not (isinstance(p, int) and p == 0):
                    act.wait_ge(stepped, STEPS * p + n - 1)
                copy(wt_hi[:, n % 2, 0:cols], ps[:, TB[n % 2], 0:cols]).then_inc(t_hi_done, 1)

            def move_o(p, unit):
                head, half = UNITS[unit]
                act.wait_ge(stepped, STEPS * p + STEP0[unit] + len(key_tiles(unit)))
                if not (isinstance(p, int) and p == 0):
                    act.wait_ge(gated_done, 4 * (p - 1) + unit + 1)
                mine = slice(head * HEAD, (head + 1) * HEAD)
                other = slice((1 - head) * HEAD, (2 - head) * HEAD)
                copy(osum[mine, half, :], ps[other, OB, :]).then_inc(o_moved, 1)

            def split_qk(p, o, h):
                cols = slice(h * HALF, (h + 1) * HALF)
                act.wait_ge(projected, 8 * p + 2 * o + HALVES[o].index(h) + 1)
                if not (isinstance(p, int) and p == 0):
                    act.wait_ge(z_done, CHUNKS * p)
                a = kk[0:HEAD, 0, cols] if o == K_ else qq[0:HEAD, 0, cols]
                b = kk[HEAD:P, 2, cols] if o == K_ else qq[HEAD:P, 1, cols]
                copy(a, ps[0:HEAD, PROJ[h], :])
                copy(b, ps[HEAD:P, PROJ[h], :]).then_inc(proj_hi_done, 1)

            def copy_v(p, h):
                act.wait_ge(projected, 8 * p + 2 * V_ + HALVES[V_].index(h) + 1)
                copy(vT[:, h * HALF:(h + 1) * HALF], ps[:, PROJ[h], :]).then_inc(bank_free[h], 1)

            def v_high(p, n):
                h = HALVES[V_][n]
                act.wait_ge(transposed, TRANS * p + n + 1)
                if n == 0 and not (isinstance(p, int) and p == 0):
                    act.wait_ge(stepped, STEPS * p)
                copy(vv[:, h * QH:(h + 1) * QH, :, 0:HEAD],
                     ps[:, TB[n % 2], :].rearrange("p (t n d) -> p t n d", t=QH, n=2)).then_inc(t_hi_done, 1)

            def gate_sigmoid(p, h):
                act.wait_ge(projected, 8 * p + 2 * G_ + h + 1)
                if h == 0 and not (isinstance(p, int) and p == 0):
                    act.wait_ge(gated_done, 4 * p)
                nc.scalar.activation(silu[:, h * HALF:(h + 1) * HALF], ps[:, PROJ[h], :],
                                     ACT.Sigmoid).then_inc(proj_hi_done, 1)

            def body(p, first=False, last=False):
                if not first:
                    for j in range(4):
                        wt_high(p - 1, 3, j)
                    move_o(p - 1, 3)
                copy_v(p, 1)
                for s in range(4):
                    sigmoids(p, 2 * s)
                    sigmoids(p, 2 * s + 1)
                    if s == 2:
                        v_high(p, 0)
                copy_v(p, 0)
                v_high(p, 1)
                for j in range(8):
                    wt_high(p, 0, j)
                    if j < 4:
                        sigmoids(p, CHUNK0[1] + j)
                    if j == 5:
                        gate_sigmoid(p, 0)
                wt_high(p, 1, 0)
                gate_sigmoid(p, 1)
                move_o(p, 0)
                for j in range(4):
                    if j:
                        wt_high(p, 1, j)
                    sigmoids(p, CHUNK0[2] + 2 * j)
                    sigmoids(p, CHUNK0[2] + 2 * j + 1)
                for j in range(8):
                    if j < 2:
                        sigmoids(p, CHUNK0[3] + 2 * j)
                    wt_high(p, 2, j)
                    if j == 0:
                        move_o(p, 1)
                    if j < 2:
                        sigmoids(p, CHUNK0[3] + 2 * j + 1)
                    if j == 1 and not last:
                        split_qk(p + 1, K_, 0)
                        split_qk(p + 1, K_, 1)
                    if j == 6 and not last:
                        split_qk(p + 1, Q_, 0)
                move_o(p, 2)
                if not last:
                    split_qk(p + 1, Q_, 1)

            for k in range(KT):
                act.wait_ge(x_loaded[k], 16)
                copy(x_hi[:, k, :], gated[:, k, :]).then_inc(x_hi_done, 1)
            for o in (K_, Q_):
                for h in range(2):
                    split_qk(0, o, h)
            body(0, first=True)
            with act.Fori(1, PAIRS - 1) as p:
                body(p)
            body(PAIRS - 1, last=True)
            for j in range(4):
                wt_high(PAIRS - 1, 3, j)
            move_o(PAIRS - 1, 3)

            def split_gated(s):
                act.wait_ge(gated_done, 4 * PAIRS)
                if s < 2:
                    act.wait_ge(z_done, CHUNKS * PAIRS)
                else:
                    act.wait_ge(y_done, s - 1)
                copy(gs[:, 2 * (s % 2), :].rearrange("p (e t) -> p e t", e=PAIRS),
                     gated[:, :, s * P:(s + 1) * P]).then_inc(gs_hi_done, 1)

            split_gated(0)
            split_gated(1)
            for s in range(ST):
                act.wait_ge(ln_step, 4 * s + 2)
                nc.scalar.activation(root[:, s % 2, 3:4], moments[:, s % 2, 2:3], ACT.Sqrt).then_inc(root_done, 1)
                if s + 2 < ST:
                    split_gated(s + 2)

        @block.vector
        def _(dve):
            def weights(p, number):
                unit = number // QH
                half = UNITS[unit][1]
                tile = half * QH + number % QH
                keys = SEQ - P * tile
                last_chunk = max(n for n, (u, t, _) in enumerate(CHUNK_LIST) if u == unit and t == tile)
                dve.wait_ge(sigmoids_done, CHUNKS * p + last_chunk + 1)
                kept = keep[:, number % 2, 0:keys]
                nc.vector.tensor_tensor_scan(kept, kept, kept, 1.0, ALU.mult, ALU.bypass).then_inc(scanned, 1)
                at = w_offset(tile)
                dve.wait_ge(scanned, TILES * p + number + 1)
                w = take[half][:, at + 1:at + keys]
                nc.vector.tensor_tensor(w, w, keep[:, number % 2, 0:keys - 1], ALU.mult).then_inc(w_ready, 1)

            def wt_low(p, unit, j):
                n = STEP0[unit] + j
                cols = min(key_tiles(unit)[j] - UNITS[unit][1] * QH + 1, QH) * P
                dve.wait_ge(t_hi_done, TRANS * p + 2 + n + 1)
                nc.vector.tensor_tensor(wt_lo[:, n % 2, 0:cols], ps[:, TB[n % 2], 0:cols],
                                        wt_hi[:, n % 2, 0:cols].bitcast(F32), ALU.subtract).then_inc(t_split, 1)

            def sum_o(p, unit):
                head, half = UNITS[unit]
                mine = slice(head * HEAD, (head + 1) * HEAD)
                dve.wait_ge(o_moved, 4 * p + unit + 1)
                nc.vector.tensor_tensor(osum[mine, half, :], ps[mine, OB, :], osum[mine, half, :],
                                        ALU.add).then_inc(o_summed, 1)

            def split_qk(p, o, h):
                cols = slice(h * HALF, (h + 1) * HALF)
                dve.wait_ge(proj_hi_done, 6 * p + 2 * o + h + 1)
                if o == K_:
                    parts = [(kk[0:HEAD, 1, cols], kk[0:HEAD, 0, cols], 0), (kk[HEAD:P, 3, cols], kk[HEAD:P, 2, cols], 1)]
                else:
                    parts = [(qq[HEAD:P, 0, cols], qq[0:HEAD, 0, cols], 0), (qq[0:HEAD, 1, cols], qq[HEAD:P, 1, cols], 1)]
                for lo, hi, head in parts:
                    op = nc.vector.tensor_tensor(lo, ps[head * HEAD:(head + 1) * HEAD, PROJ[h], :],
                                                 hi.bitcast(F32), ALU.subtract)
                op.then_inc(bank_free[h], 1)

            def v_low(p, n):
                h = HALVES[V_][n]
                dve.wait_ge(t_hi_done, TRANS * p + n + 1)
                tiles = slice(h * QH, (h + 1) * QH)
                nc.vector.tensor_tensor(vv[:, tiles, :, HEAD:2 * HEAD],
                                        ps[:, TB[n % 2], :].rearrange("p (t n d) -> p t n d", t=QH, n=2),
                                        vv[:, tiles, :, 0:HEAD].bitcast(F32), ALU.subtract).then_inc(t_split, 1)

            def gate(p, h):
                dve.wait_ge(proj_hi_done, 6 * p + 4 + h + 1)
                half = silu[:, h * HALF:(h + 1) * HALF]
                nc.vector.tensor_tensor(half, ps[:, PROJ[h], :], half, ALU.mult).then_inc(bank_free[h], 1)

            def body(p, first=False, last=False):
                if not first:
                    for j in range(4):
                        wt_low(p - 1, 3, j)
                    sum_o(p - 1, 3)
                for s in range(4):
                    weights(p, s)
                    if s == 2:
                        v_low(p, 0)
                v_low(p, 1)
                for j in range(8):
                    wt_low(p, 0, j)
                    if j < 4:
                        weights(p, TILE0[1] + j)
                    if j == 5:
                        gate(p, 0)
                wt_low(p, 1, 0)
                gate(p, 1)
                sum_o(p, 0)
                for j in range(4):
                    if j:
                        wt_low(p, 1, j)
                    weights(p, TILE0[2] + j)
                for j in range(8):
                    wt_low(p, 2, j)
                    if j == 0:
                        sum_o(p, 1)
                    if j < 2:
                        weights(p, TILE0[3] + 2 * j)
                        weights(p, TILE0[3] + 2 * j + 1)
                    if j == 1 and not last:
                        split_qk(p + 1, K_, 0)
                        split_qk(p + 1, K_, 1)
                    if j == 6 and not last:
                        split_qk(p + 1, Q_, 0)
                sum_o(p, 2)
                if not last:
                    split_qk(p + 1, Q_, 1)

            for k in range(KT):
                dve.wait_ge(x_hi_done, k + 1)
                nc.vector.tensor_tensor(x_lo[:, k, :], gated[:, k, :], x_hi[:, k, :].bitcast(F32),
                                        ALU.subtract).then_inc(x_lo_done, 1)
            for o in (K_, Q_):
                for h in range(2):
                    split_qk(0, o, h)
            body(0, first=True)
            with dve.Fori(1, PAIRS - 1) as p:
                body(p)
            body(PAIRS - 1, last=True)
            for j in range(4):
                wt_low(PAIRS - 1, 3, j)
            sum_o(PAIRS - 1, 3)

            def split_gated(s):
                dve.wait_ge(gs_hi_done, s + 1)
                nc.vector.tensor_tensor(gs[:, 2 * (s % 2) + 1, :].rearrange("p (e t) -> p e t", e=PAIRS),
                                        gated[:, :, s * P:(s + 1) * P],
                                        gs[:, 2 * (s % 2), :].bitcast(F32).rearrange("p (e t) -> p e t", e=PAIRS),
                                        ALU.subtract).then_inc(gs_split, 1)

            split_gated(0)
            split_gated(1)
            for s in range(ST):
                b = s % 2
                m = moments[:, b, :]
                mean, var, vare, rt, r0, t0 = (m[:, i:i + 1] for i in range(6))
                dve.wait_ge(y_done, s + 1)
                dve.wait_ge(res_loaded[b], 16 * (s // 2 + 1))
                if s == 0:
                    dve.wait_ge(lnp_loaded, 32)
                t = yt[b]
                nc.vector.scalar_tensor_tensor(
                    t.rearrange("p (n d) -> p n d", n=2), res[b].rearrange("p (n d) -> p n d", n=2), ALPHA,
                    ps[:, 2 * b:2 * b + 2, :], ALU.mult, ALU.add).then_inc(y_read, 1)
                dve.wait_ge(y_read, s + 1)
                for h in range(2):
                    op = nc.vector.bn_stats(stats[:, b, h, :], t[:, h * HALF:(h + 1) * HALF])
                op.then_inc(scaled, 1)
                dve.wait_ge(scaled, 6 * s + 1)
                nc.vector.bn_aggr(m[:, 0:2], stats[:, b, :, :]).then_inc(ln_step, 1)
                dve.wait_ge(ln_step, 4 * s + 1)
                nc.vector.tensor_scalar(vare, var, EPS, None, ALU.add).then_inc(ln_step, 1)
                if s + 2 < ST:
                    split_gated(s + 2)
                dve.wait_ge(root_done, s + 1)
                nc.vector.reciprocal(r0, rt).then_inc(ln_step, 1)
                dve.wait_ge(ln_step, 4 * s + 3)
                nc.vector.tensor_scalar(t0, vare, r0, r0, ALU.mult, ALU.mult).then_inc(scaled, 1)
                dve.wait_ge(scaled, 6 * s + 2)
                nc.vector.tensor_scalar(t0, t0, -0.5, 1.5, ALU.mult, ALU.add).then_inc(scaled, 1)
                dve.wait_ge(scaled, 6 * s + 3)
                nc.vector.tensor_tensor(r0, r0, t0, ALU.mult).then_inc(ln_step, 1)
                dve.wait_ge(ln_step, 4 * s + 4)
                nc.vector.tensor_scalar(t, t, mean, r0, ALU.subtract, ALU.mult).then_inc(scaled, 1)
                dve.wait_ge(scaled, 6 * s + 4)
                nc.vector.tensor_tensor(t, t, ln_par[:, 0, :], ALU.mult).then_inc(scaled, 1)
                dve.wait_ge(scaled, 6 * s + 5)
                nc.vector.tensor_tensor(res[b], t, ln_par[:, 1, :], ALU.add).then_inc(normed, 1)
                dve.wait_ge(normed, s + 1)
                nc.vector.tensor_copy(t0, t0).then_inc(scaled, 1)

        @block.gpsimd
        def _(pool):
            def split_w(p, o, gates=None):
                if gates is not None:
                    pool.wait_ge(gated_done, gates)
                pool.wait_ge(w_loaded[o], 16 * (p + 1))
                if not (isinstance(p, int) and p == 0 and o < 2):
                    pool.wait_ge(projected, 8 * p + 2 * o - 2)
                nc.gpsimd.tensor_tensor(w_hi[:, o % 2, :], w_raw[:, o, :], ones[:, 0:1].broadcast_to([P, KT * P]),
                                        ALU.mult).then_inc(w_hi_done, 1)
                pool.wait_ge(w_hi_done, 4 * p + o + 1)
                nc.gpsimd.tensor_tensor(w_lo[:, o % 2, :], w_raw[:, o, :], w_hi[:, o % 2, :].bitcast(F32),
                                        ALU.subtract).then_inc(w_split, 1)

            def gate_o(p, unit, splits):
                head, half = UNITS[unit]
                pool.wait_ge(w_split, splits)
                if unit or not (isinstance(p, int) and p == 0):
                    pool.wait_ge(gated_done, 4 * p + unit)
                mine = slice(head * HEAD, (head + 1) * HEAD)
                cols = slice(half * HALF, (half + 1) * HALF)
                pool.wait_ge(o_summed, 4 * p + unit + 1)
                pool.wait_ge(bank_free[half], 4 * p + G_ + 1)
                nc.gpsimd.tensor_tensor(gated[mine, p, cols], osum[mine, half, :], silu[mine, cols],
                                        ALU.mult).then_inc(gated_done, 1)

            def body(p, first=False, last=False):
                split_w(p, G_, None if first else 4 * p - 1)
                if not first:
                    gate_o(p - 1, 3, 4 * p + 4)
                if not last:
                    split_w(p + 1, K_, None if first else 4 * p)
                gate_o(p, 0, 4 * p + (4 if last else 5))
                if not last:
                    split_w(p + 1, Q_, 4 * p + 1)
                gate_o(p, 1, 4 * p + (4 if last else 6))
                if not last:
                    split_w(p + 1, V_, 4 * p + 2)
                gate_o(p, 2, 4 * p + (4 if last else 7))

            nc.gpsimd.memset(ones[:, :], 1.0).then_inc(ones_set, 1)
            pool.wait_ge(ones_set, 1)
            split_w(0, K_)
            split_w(0, Q_)
            split_w(0, V_)
            body(0, first=True)
            with pool.Fori(1, PAIRS - 1) as p:
                body(p)
            body(PAIRS - 1, last=True)

            def split_wo(e):
                pool.wait_ge(wo_loaded[e // 4], 16)
                if e == 0:
                    pool.wait_ge(projected, 8 * PAIRS)
                    pool.wait_ge(gated_done, 4 * PAIRS - 1)
                nc.gpsimd.tensor_copy(wo_hi[:, e, :], w_raw[:, e % 4, :]).then_inc(wo_hi_done, 1)
                pool.wait_ge(wo_hi_done, e + 1)
                nc.gpsimd.tensor_tensor(wo_lo[:, e, :], w_raw[:, e % 4, :], wo_hi[:, e, :].bitcast(F32),
                                        ALU.subtract).then_inc(wo_split, 1)

            for e in range(PAIRS):
                split_wo(e)
            pool.wait_ge(wo_split, PAIRS)
            gate_o(PAIRS - 1, 3, 4 * PAIRS)


def kernel(x, w_in, w_out, ln_g, ln_b, rel_table):
    import concourse.bacc as bacc
    import ml_dtypes
    import numpy as np
    from concourse.bass_utils import run_bass_kernel_spmd

    x, w_in, w_out = np.asarray(x), np.asarray(w_in), np.asarray(w_out)
    rows = x[0, ::-1]
    w = w_in[0].reshape(KT, P, 4, PAIRS, P)[:, :, [1, 0, 2, 3]].transpose(3, 2, 1, 0, 4)
    one = np.eye(P, dtype=np.float32)
    not_past = np.where(np.arange(P)[None, :] <= np.arange(P)[:, None], np.float32(MASKED), np.float32(0))
    arrays = {
        "xT": rows.T.reshape(KT, P, SEQ),
        "x_rows": rows.reshape(ST, P, DM),
        "w_in": w.reshape(PAIRS, 4, P, KT * P),
        "w_out": w_out[0].reshape(2, 4, P, DM).transpose(0, 2, 1, 3),
        "ln_g": np.asarray(ln_g),
        "ln_b": np.asarray(ln_b),
        "consts_f": one,
        "consts_b": np.stack([one, not_past], axis=1).astype(ml_dtypes.bfloat16),
    }
    arrays = {f"in_{n}": np.ascontiguousarray(a) for n, a in arrays.items()}
    nc = bacc.Bacc("TRN2", target_bir_lowering=False, num_devices=1)
    args = [nc.dram_tensor(n, a.shape, mybir.dt.from_np(a.dtype), kind="ExternalInput").ap()
            for n, a in arrays.items()]
    args.append(nc.dram_tensor("out_y", (ST, P, DM), F32, kind="ExternalOutput").ap())
    stick_breaking_layer(nc, *args)
    r = run_bass_kernel_spmd(nc, [arrays], core_ids=[0])
    y = np.asarray(r.results[0]["out_y"])
    return y.reshape(1, SEQ, DM)[:, ::-1]
```

```python
from contextlib import ExitStack

import concourse.bass as bass
from concourse import mybir

F32 = mybir.dt.float32
F32R = mybir.dt.float32r
BF16 = mybir.dt.bfloat16
ALU = mybir.AluOpType
ACT = mybir.ActivationFunctionType

P = 128
SEQ = 1024
DM = 1024
HEAD = 64
PAIRS = 8
KT = DM // P
ST = SEQ // P
HALF = SEQ // 2
QH = ST // 2
SCALE = float(HEAD) ** -0.5
ALPHA = 2.0 ** 0.25
EPS = 1e-5
MASKED = -1e30

KEEPS = 4
POOL_WO = 5

K_, Q_, V_, G_ = range(4)
HALVES = (1, 0)

PROJ = (0, 1)
ZB = (2, 3, 4)
TB = (5, 6)
OB = 7

CHUNKS = 24
TILES = 16
STEPS = 24
TRANS = 2 + STEPS

UNITS = [(0, 0), (0, 1), (1, 0), (1, 1)]
CHUNK0 = [0, 8, 12, 20]
TILE0 = [0, 4, 8, 12]
STEP0 = [0, 8, 12, 20]


def chunks_of(tile):
    first = P * tile
    keys = SEQ - first
    return [(first, min(keys, HALF))] + ([(first + HALF, keys - HALF)] if keys > HALF else [])


CHUNK_LIST = [(u, half * QH + i, c) for u, (_, half) in enumerate(UNITS) for i in range(QH)
              for c in range(len(chunks_of(half * QH + i)))]


def w_offset(tile):
    half = tile // QH
    return sum(SEQ - P * t for t in range(half * QH, tile))


W_SIZE = [w_offset(QH - 1) + SEQ - P * (QH - 1), w_offset(ST - 1) + SEQ - P * (ST - 1)]


def key_tiles(unit):
    return list(range(ST - 1, UNITS[unit][1] * QH - 1, -1))


def stick_breaking_layer(nc, xT, x_rows, w_in, w_out, ln_g, ln_b, consts_f, consts_b, out):
    with ExitStack() as ctx:
        def sb(name, shape, dt=F32):
            return ctx.enter_context(nc.sbuf_tensor(name, shape, dt))

        def sem(name):
            return ctx.enter_context(nc.semaphore(name))

        ps = ctx.enter_context(nc.psum_tensor("ps", [P, 8, HALF], F32))

        x_hi = sb("x_hi", [P, KT, SEQ], F32R)
        x_lo = sb("x_lo", [P, KT, SEQ], F32R)
        w_raw = sb("w_raw", [P, 2, KT * P])
        w_hi = sb("w_hi", [P, 2, KT * P], F32R)
        w_lo = sb("w_lo", [P, 2, KT * P], F32R)
        kk = sb("kk", [P, 4, SEQ], F32R)
        qq = sb("qq", [P, 2, SEQ], F32R)
        vT = sb("vT", [P, SEQ])
        vv = sb("vv", [P, ST, 2, 2 * HEAD], F32R)
        gated = sb("gated", [P, PAIRS, SEQ])
        silu = sb("silu", [P, SEQ])
        take = [sb(f"take{h}", [P, W_SIZE[h]]) for h in range(2)]
        keep = sb("keep", [P, KEEPS, SEQ])
        wt_hi = sb("wt_hi", [P, 2, HALF], F32R)
        wt_lo = sb("wt_lo", [P, 2, HALF], F32R)
        osum = sb("osum", [P, 2, HALF])
        ident = sb("ident", [P, P])
        ident_b = sb("ident_b", [P, 2, P], BF16)
        ones = sb("ones", [P, 1])
        stats = sb("stats", [P, 2, 2, 6])
        moments = sb("moments", [P, 2, 8])

        x_loaded = [sem(f"x_loaded{k}") for k in range(KT)]
        consts_loaded = sem("consts_loaded")
        w_loaded = [sem("w_loaded0"), sem("w_loaded1")]
        k_copied = sem("k_copied")
        ones_set = sem("ones_set")
        x_hi_done = sem("x_hi_done")
        x_lo_done = sem("x_lo_done")
        w0_hi_done = sem("w0_hi_done")
        w0_lo_done = sem("w0_lo_done")
        w_hi_done = sem("w_hi_done")
        w_split = sem("w_split")
        projected = sem("projected")
        proj_hi_done = sem("proj_hi_done")
        bank_free = [sem("bank_free0"), sem("bank_free1")]
        z_done = sem("z_done")
        sigmoids_done = sem("sigmoids_done")
        scanned = sem("scanned")
        w_ready = sem("w_ready")
        transposed = sem("transposed")
        t_hi_done = sem("t_hi_done")
        t_split = sem("t_split")
        stepped = sem("stepped")
        o_moved = sem("o_moved")
        o_summed = sem("o_summed")
        gated_done = sem("gated_done")
        wo_hi_done = sem("wo_hi_done")
        wo_split = sem("wo_split")
        wo_hi_done_act = sem("wo_hi_done_act")
        wo_split_dve = sem("wo_split_dve")
        gs_hi_done = sem("gs_hi_done")
        gs_split = sem("gs_split")
        lnp_loaded = sem("lnp_loaded")
        res_loaded = [sem("res_loaded0"), sem("res_loaded1")]
        y_done = sem("y_done")
        ln_step = sem("ln_step")
        root_done = sem("root_done")
        y_read = sem("y_read")
        scaled = sem("scaled")
        normed = sem("normed")
        stored = [sem("stored0"), sem("stored1")]

        wo_hi, wo_lo = x_hi, x_lo
        gs_hi, gs_lo = w_hi, w_lo
        ln_par = keep
        take0 = take[0][:, 0:2 * DM].rearrange("p (n d) -> p n d", n=2)
        res = [take0[:, 0, :], take0[:, 1, :]]
        yt = [keep[:, 2, :], keep[:, 3, :]]
        root = moments

        block = ctx.enter_context(nc.Block())

        @block.sync
        def _(sp):
            def load_w(p, o):
                sp.dma_start(w_raw[:, o % 2, :], w_in[p, o]).then_inc(w_loaded[o % 2], 16)

            load_w(0, K_)
            for k in range(KT):
                sp.dma_start(gated[:, k, :], xT[k]).then_inc(x_loaded[k], 16)
                if k == 3:
                    load_w(0, Q_)
            sp.dma_start(ident[:, :], consts_f).then_inc(consts_loaded, 16)
            sp.dma_start(ident_b[:, :, :], consts_b).then_inc(consts_loaded, 16)
            sp.wait_ge(w0_lo_done, 1)
            load_w(0, V_)
            sp.wait_ge(w_split, 1)
            load_w(0, G_)

            def duplicate_k(p):
                for h in range(2):
                    sp.wait_ge(bank_free[h], 4 * p + K_ + 1)
                sp.dma_start(kk[HEAD:P, 0:2, :].bitcast(F32), kk[0:HEAD, 0:2, :].bitcast(F32)).then_inc(k_copied, 16)
                sp.dma_start(kk[0:HEAD, 2:4, :].bitcast(F32), kk[HEAD:P, 2:4, :].bitcast(F32)).then_inc(k_copied, 16)

            def body(p):
                for o in (K_, Q_, V_, G_):
                    sp.wait_ge(w_split, 4 * p + o + 2)
                    load_w(p + 1, o)
                duplicate_k(p + 1)

            duplicate_k(0)
            body(0)
            with sp.Fori(1, PAIRS - 1) as p:
                body(p)

            for e in range(PAIRS):
                if e < 2:
                    sp.wait_ge(w_split, 4 * PAIRS - 2 + e)
                elif e - 2 < POOL_WO:
                    sp.wait_ge(wo_split, e - 1)
                else:
                    sp.wait_ge(wo_split_dve, e - 2 - POOL_WO + 1)
                sp.dma_start(w_raw[:, e % 2, :], w_out[e]).then_inc(w_loaded[e % 2], 16)
            sp.wait_ge(w_ready, TILES * PAIRS)
            sp.dma_start(ln_par[:, 0, :], ln_g.broadcast_to([P, DM])).then_inc(lnp_loaded, 16)
            sp.dma_start(ln_par[:, 1, :], ln_b.broadcast_to([P, DM])).then_inc(lnp_loaded, 16)
            sp.wait_ge(transposed, TRANS * (PAIRS - 1) + 2 + STEP0[3])
            for s in range(2):
                sp.dma_start(res[s], x_rows[s]).then_inc(res_loaded[s], 16)
            for s in range(ST):
                sp.wait_ge(normed, s + 1)
                sp.dma_start(out[s], res[s % 2]).then_inc(stored[s % 2], 16)
                if s + 2 < ST:
                    sp.wait_ge(stored[s % 2], 16 * (s // 2 + 1))
                    sp.dma_start(res[s % 2], x_rows[s + 2]).then_inc(res_loaded[s % 2], 16)
            for b in range(2):
                sp.wait_ge(stored[b], 16 * (ST // 2))

        @block.tensor
        def _(pe):
            def project(p, o, first, count):
                for m in range(first, first + count):
                    n, k, part = m // (3 * KT), m // 3 % KT, m % 3
                    h = HALVES[n]
                    if m == 0:
                        pe.wait_ge(w_split, 4 * p + o)
                    if m % (3 * KT) == 0:
                        pe.wait_ge(bank_free[h], 4 * p + o)
                    project_part(o, h, k, part)

            def project_part(o, h, k, part):
                w = (w_hi, w_hi, w_lo)[part][:, o % 2, k * P:(k + 1) * P]
                x = (x_hi, x_lo, x_hi)[part][:, k, h * HALF:(h + 1) * HALF]
                last = k == KT - 1 and part == 2
                mm = nc.tensor.matmul(ps[:, PROJ[h], :], w, x, start=(k == 0 and part == 0), stop=last)
                if last:
                    mm.then_inc(projected, 1)

            def scores(p, n):
                unit, tile, c = CHUNK_LIST[n]
                head = UNITS[unit][0]
                key, keys = chunks_of(tile)[c]
                if n in (0, CHUNK0[2]):
                    pe.wait_ge(k_copied, 32 * (p + 1))
                    for h in range(2):
                        pe.wait_ge(bank_free[h], 4 * p + Q_ + 1)
                if n >= len(ZB) or not (isinstance(p, int) and p == 0):
                    pe.wait_ge(sigmoids_done, CHUNKS * p + n - len(ZB) + 1)
                z = ps[:, ZB[n % len(ZB)], 0:keys]
                q = qq[:, head, tile * P:(tile + 1) * P]
                nc.tensor.matmul(z, q, kk[:, 2 * head, key:key + keys], start=True, stop=False)
                if c == 0:
                    nc.tensor.matmul(z[:, 0:P], ident_b[:, 0, :], ident_b[:, 1, :], start=False, stop=False)
                nc.tensor.matmul(z, q, kk[:, 2 * head + 1, key:key + keys], start=False,
                                 stop=True).then_inc(z_done, 1)

            def transpose_v(p, n):
                h = HALVES[n]
                pe.wait_ge(bank_free[h], 4 * p + V_ + 1)
                if not (isinstance(p, int) and p == 0):
                    pe.wait_ge(t_split, TRANS * p + n - 1)
                for i in range(QH):
                    t = h * QH + i
                    mm = nc.tensor.transpose(ps[:, TB[n % 2], i * P:(i + 1) * P], vT[:, t * P:(t + 1) * P],
                                             ident[:, :])
                mm.then_inc(transposed, 1)

            def transpose_w(p, unit, j):
                head, half = UNITS[unit]
                tile = key_tiles(unit)[j]
                if j == 0:
                    pe.wait_ge(w_ready, TILES * p + TILE0[unit] + QH)
                n = STEP0[unit] + j
                pe.wait_ge(t_split, TRANS * p + 2 + n - 1)
                for i in range(min(tile - half * QH + 1, QH)):
                    q = half * QH + i
                    at = w_offset(q) + (tile - q) * P
                    mm = nc.tensor.transpose(ps[:, TB[n % 2], i * P:(i + 1) * P], take[half][:, at:at + P],
                                             ident[:, :])
                mm.then_inc(transposed, 1)

            def values(p, unit, j):
                head, half = UNITS[unit]
                tile = key_tiles(unit)[j]
                n = STEP0[unit] + j
                pe.wait_ge(t_split, TRANS * p + 2 + n + 1)
                if j == 0 and not (unit == 0 and isinstance(p, int) and p == 0):
                    pe.wait_ge(o_summed, 4 * p + unit)
                cols = min(tile - half * QH + 1, QH) * P
                last = j == len(key_tiles(unit)) - 1
                nc.tensor.matmul(ps[:, OB, 0:cols], vv[:, tile, head, :], wt_hi[:, n % 2, 0:cols],
                                 start=(j == 0), stop=False)
                nc.tensor.matmul(ps[:, OB, 0:cols], vv[:, tile, head, :], wt_lo[:, n % 2, 0:cols],
                                 start=False, stop=last).then_inc(stepped, 1)

            def output(s, e):
                if s < 2 and e == 0:
                    pe.wait_ge(gs_split, s + 1)
                    if s == 0:
                        for h in range(2):
                            pe.wait_ge(bank_free[h], 4 * PAIRS)
                    else:
                        pe.wait_ge(sigmoids_done, CHUNKS * PAIRS - 1)
                elif s < 2 and e == PAIRS - 1:
                    pe.wait_ge(gs_split, 2 + s + 1)
                elif e == 0:
                    pe.wait_ge(gs_split, 2 + s + 1)
                    pe.wait_ge(y_read, s - 1)
                if s == 0:
                    if e < POOL_WO:
                        pe.wait_ge(wo_split, e + 1)
                    else:
                        pe.wait_ge(wo_split_dve, e - POOL_WO + 1)
                for h in range(2):
                    for part in range(3):
                        a = (gs_hi, gs_hi, gs_lo)[part][:, s % 2, e * P:(e + 1) * P]
                        b = (wo_hi, wo_lo, wo_hi)[part][:, e, h * HALF:(h + 1) * HALF]
                        mm = nc.tensor.matmul(ps[:, 2 * (s % 2) + h, :], a, b, start=(e == 0 and part == 0),
                                              stop=(e == PAIRS - 1 and part == 2))
                if e == PAIRS - 1:
                    mm.then_inc(y_done, 1)

            def last_unit_tail(p, fill):
                for j in range(4):
                    transpose_w(p, 3, j)
                    fill(j)
                    if j:
                        values(p, 3, j - 1)
                values(p, 3, 3)

            def body(p, first=False, last=False):
                if first:
                    project(p, V_, 0, 32)
                else:
                    last_unit_tail(p - 1, lambda j: project(p, V_, 8 * j, 8))
                for s in range(4):
                    scores(p, 2 * s)
                    project(p, V_, 32 + 4 * s, 2)
                    scores(p, 2 * s + 1)
                    project(p, V_, 34 + 4 * s, 2)
                    if s == 1:
                        transpose_v(p, 0)
                project(p, G_, 0, 8)
                transpose_v(p, 1)
                scores(p, CHUNK0[1])
                project(p, G_, 8, 8)
                for j in range(8):
                    transpose_w(p, 0, j)
                    if 0 < j < 4:
                        scores(p, CHUNK0[1] + j)
                    project(p, G_, 16 + 4 * j, 4)
                    if j:
                        values(p, 0, j - 1)
                for j in range(4):
                    transpose_w(p, 1, j)
                    if j == 0:
                        values(p, 0, 7)
                    else:
                        values(p, 1, j - 1)
                    for c in range(2):
                        scores(p, CHUNK0[2] + 2 * j + c)
                        if not last:
                            project(p + 1, K_, 6 * j + 3 * c, 3)
                scores(p, CHUNK0[3])
                if not last:
                    project(p + 1, K_, 24, 3)
                scores(p, CHUNK0[3] + 1)
                if not last:
                    project(p + 1, K_, 27, 3)
                values(p, 1, 3)
                for j in range(8):
                    transpose_w(p, 2, j)
                    if j < 2:
                        scores(p, CHUNK0[3] + 2 + j)
                    if last:
                        if j < 7:
                            output(0, j)
                        if j >= 3:
                            output(1, j - 3)
                    elif j < 3:
                        project(p + 1, K_, 30 + 6 * j, 6)
                    else:
                        project(p + 1, Q_, 10 * (j - 3), 10 if j < 7 else 8)
                    if j:
                        values(p, 2, j - 1)
                values(p, 2, 7)

            pe.wait_ge(w0_lo_done, 1)
            for k in range(KT):
                pe.wait_ge(x_lo_done, k + 1)
                for h in HALVES:
                    for part in range(3):
                        project_part(K_, h, k, part)
            project(0, Q_, 0, 48)
            pe.wait_ge(consts_loaded, 32)
            body(0, first=True)
            with pe.Fori(1, PAIRS - 1) as p:
                body(p)
            body(PAIRS - 1, last=True)
            last_unit_tail(PAIRS - 1, lambda j: output(*((1, 5), (1, 6), (0, 7), (1, 7))[j]))

            for s in range(2, ST):
                for e in range(PAIRS):
                    output(s, e)

        @block.scalar
        def _(act):
            def copy(dst, src):
                return nc.scalar.activation(dst, src, ACT.Copy)

            def sigmoids(p, n):
                unit, tile, c = CHUNK_LIST[n]
                half = UNITS[unit][1]
                key, keys = chunks_of(tile)[c]
                number = TILE0[unit] + tile - half * QH
                act.wait_ge(z_done, CHUNKS * p + n + 1)
                if c == 0 and (number >= KEEPS or not (isinstance(p, int) and p == 0)):
                    act.wait_ge(w_ready, TILES * p + number - KEEPS + 1)
                if n == CHUNK0[unit] and (unit >= 2 or not (isinstance(p, int) and p == 0)):
                    before = STEP0[unit - 1] if unit >= 2 else STEP0[unit + 2] + (8, 4)[half] - TRANS
                    act.wait_ge(transposed, TRANS * p + 2 + before)
                z = ps[:, ZB[n % len(ZB)], 0:keys]
                off = key - P * tile
                nc.scalar.activation(keep[:, number % KEEPS, off:off + keys], z, ACT.Sigmoid, scale=-SCALE)
                at = w_offset(tile) + off
                nc.scalar.activation(take[half][:, at:at + keys], z, ACT.Sigmoid,
                                     scale=SCALE).then_inc(sigmoids_done, 1)

            def wt_high(p, unit, j):
                n = STEP0[unit] + j
                cols = min(key_tiles(unit)[j] - UNITS[unit][1] * QH + 1, QH) * P
                act.wait_ge(transposed, TRANS * p + 2 + n + 1)
                if n >= 2 or not (isinstance(p, int) and p == 0):
                    act.wait_ge(stepped, STEPS * p + n - 1)
                copy(wt_hi[:, n % 2, 0:cols], ps[:, TB[n % 2], 0:cols]).then_inc(t_hi_done, 1)

            def move_o(p, unit):
                head, half = UNITS[unit]
                act.wait_ge(stepped, STEPS * p + STEP0[unit] + len(key_tiles(unit)))
                if not (isinstance(p, int) and p == 0):
                    act.wait_ge(gated_done, 4 * (p - 1) + unit + 1)
                mine = slice(head * HEAD, (head + 1) * HEAD)
                other = slice((1 - head) * HEAD, (2 - head) * HEAD)
                copy(osum[mine, half, :], ps[other, OB, :]).then_inc(o_moved, 1)

            def split_qk(p, o, h):
                cols = slice(h * HALF, (h + 1) * HALF)
                act.wait_ge(projected, 8 * p + 2 * o + HALVES.index(h) + 1)
                if not (isinstance(p, int) and p == 0):
                    act.wait_ge(z_done, CHUNKS * p)
                a = kk[0:HEAD, 0, cols] if o == K_ else qq[0:HEAD, 0, cols]
                b = kk[HEAD:P, 2, cols] if o == K_ else qq[HEAD:P, 1, cols]
                copy(a, ps[0:HEAD, PROJ[h], :])
                copy(b, ps[HEAD:P, PROJ[h], :]).then_inc(proj_hi_done, 1)

            def copy_v(p, h):
                act.wait_ge(projected, 8 * p + 2 * V_ + HALVES.index(h) + 1)
                copy(vT[:, h * HALF:(h + 1) * HALF], ps[:, PROJ[h], :]).then_inc(bank_free[h], 1)

            def v_high(p, n):
                h = HALVES[n]
                act.wait_ge(transposed, TRANS * p + n + 1)
                if n == 0 and not (isinstance(p, int) and p == 0):
                    act.wait_ge(stepped, STEPS * p)
                copy(vv[:, h * QH:(h + 1) * QH, :, 0:HEAD],
                     ps[:, TB[n % 2], :].rearrange("p (t n d) -> p t n d", t=QH, n=2)).then_inc(t_hi_done, 1)

            def gate_sigmoid(p, h):
                act.wait_ge(projected, 8 * p + 2 * G_ + HALVES.index(h) + 1)
                if h == HALVES[0] and not (isinstance(p, int) and p == 0):
                    act.wait_ge(gated_done, 4 * p)
                nc.scalar.activation(silu[:, h * HALF:(h + 1) * HALF], ps[:, PROJ[h], :],
                                     ACT.Sigmoid).then_inc(proj_hi_done, 1)

            def split_gated(s, first, end):
                if end < PAIRS:
                    act.wait_ge(gated_done, 4 * end)
                    act.wait_ge(projected, 8 * PAIRS)
                else:
                    act.wait_ge(gated_done, 4 * PAIRS - (1 if s < QH else 0))
                if s >= 2:
                    act.wait_ge(y_done, s - 1)
                copy(gs_hi[:, s % 2, first * P:end * P].rearrange("p (e t) -> p e t", t=P),
                     gated[:, first:end, s * P:(s + 1) * P]).then_inc(gs_hi_done, 1)

            def split_wo(e):
                act.wait_ge(w_loaded[e % 2], 16 * (2 * PAIRS + e // 2 + 1))
                copy(wo_hi[:, e, :], w_raw[:, e % 2, :]).then_inc(wo_hi_done_act, 1)

            def body(p, first=False, last=False):
                if not first:
                    for j in range(4):
                        wt_high(p - 1, 3, j)
                    move_o(p - 1, 3)
                copy_v(p, 1)
                for s in range(4):
                    sigmoids(p, 2 * s)
                    sigmoids(p, 2 * s + 1)
                    if s == 2:
                        v_high(p, 0)
                copy_v(p, 0)
                v_high(p, 1)
                sigmoids(p, CHUNK0[1])
                for j in range(8):
                    wt_high(p, 0, j)
                    if 0 < j < 4:
                        sigmoids(p, CHUNK0[1] + j)
                    if j == 3:
                        gate_sigmoid(p, 1)
                for j in range(4):
                    wt_high(p, 1, j)
                    if j == 0:
                        move_o(p, 0)
                        gate_sigmoid(p, 0)
                    sigmoids(p, CHUNK0[2] + 2 * j)
                    sigmoids(p, CHUNK0[2] + 2 * j + 1)
                    if last and j < 2:
                        split_gated(j, 0, PAIRS - 1)
                for c in range(2):
                    sigmoids(p, CHUNK0[3] + c)
                move_o(p, 1)
                for j in range(8):
                    wt_high(p, 2, j)
                    if j < 2:
                        sigmoids(p, CHUNK0[3] + 2 + j)
                    if last:
                        if j in (3, 5, 6):
                            split_wo((3, 5, 6).index(j) + POOL_WO)
                    elif j == 1:
                        split_qk(p + 1, K_, 1)
                    elif j == 3:
                        split_qk(p + 1, K_, 0)
                    elif j == 6:
                        split_qk(p + 1, Q_, 1)
                move_o(p, 2)
                if not last:
                    split_qk(p + 1, Q_, 0)

            act.wait_ge(w_loaded[0], 16)
            copy(w_hi[:, 0, :], w_raw[:, K_, :]).then_inc(w0_hi_done, 1)
            for k in range(KT):
                act.wait_ge(x_loaded[k], 16)
                copy(x_hi[:, k, :], gated[:, k, :]).then_inc(x_hi_done, 1)
            for o in (K_, Q_):
                for h in HALVES:
                    split_qk(0, o, h)
            body(0, first=True)
            with act.Fori(1, PAIRS - 1) as p:
                body(p)
            body(PAIRS - 1, last=True)
            for j in range(4):
                wt_high(PAIRS - 1, 3, j)
                if j == 1:
                    split_gated(0, PAIRS - 1, PAIRS)
                    split_gated(1, PAIRS - 1, PAIRS)
            move_o(PAIRS - 1, 3)
            for s in range(ST):
                if s + 2 < ST:
                    split_gated(s + 2, 0, PAIRS)
                act.wait_ge(ln_step, 4 * s + 2)
                nc.scalar.activation(root[:, s % 2, 3:4], moments[:, s % 2, 2:3], ACT.Sqrt).then_inc(root_done, 1)

        @block.vector
        def _(dve):
            def weights(p, number):
                unit = number // QH
                half = UNITS[unit][1]
                tile = half * QH + number % QH
                keys = SEQ - P * tile
                last_chunk = max(n for n, (u, t, _) in enumerate(CHUNK_LIST) if u == unit and t == tile)
                dve.wait_ge(sigmoids_done, CHUNKS * p + last_chunk + 1)
                kept = keep[:, number % KEEPS, 0:keys]
                nc.vector.tensor_tensor_scan(kept, kept, kept, 1.0, ALU.mult, ALU.bypass).then_inc(scanned, 1)
                at = w_offset(tile)
                dve.wait_ge(scanned, TILES * p + number + 1)
                w = take[half][:, at + 1:at + keys]
                nc.vector.tensor_tensor(w, w, keep[:, number % KEEPS, 0:keys - 1], ALU.mult).then_inc(w_ready, 1)

            def wt_low(p, unit, j):
                n = STEP0[unit] + j
                cols = min(key_tiles(unit)[j] - UNITS[unit][1] * QH + 1, QH) * P
                dve.wait_ge(t_hi_done, TRANS * p + 2 + n + 1)
                nc.vector.tensor_tensor(wt_lo[:, n % 2, 0:cols], ps[:, TB[n % 2], 0:cols],
                                        wt_hi[:, n % 2, 0:cols].bitcast(F32), ALU.subtract).then_inc(t_split, 1)

            def sum_o(p, unit):
                head, half = UNITS[unit]
                mine = slice(head * HEAD, (head + 1) * HEAD)
                dve.wait_ge(o_moved, 4 * p + unit + 1)
                nc.vector.tensor_tensor(osum[mine, half, :], ps[mine, OB, :], osum[mine, half, :],
                                        ALU.add).then_inc(o_summed, 1)

            def split_qk(p, o, h):
                cols = slice(h * HALF, (h + 1) * HALF)
                dve.wait_ge(proj_hi_done, 6 * p + 2 * o + HALVES.index(h) + 1)
                if o == K_:
                    parts = [(kk[0:HEAD, 1, cols], kk[0:HEAD, 0, cols], 0), (kk[HEAD:P, 3, cols], kk[HEAD:P, 2, cols], 1)]
                else:
                    parts = [(qq[HEAD:P, 0, cols], qq[0:HEAD, 0, cols], 0), (qq[0:HEAD, 1, cols], qq[HEAD:P, 1, cols], 1)]
                for lo, hi, head in parts:
                    op = nc.vector.tensor_tensor(lo, ps[head * HEAD:(head + 1) * HEAD, PROJ[h], :],
                                                 hi.bitcast(F32), ALU.subtract)
                op.then_inc(bank_free[h], 1)

            def v_low(p, n):
                h = HALVES[n]
                dve.wait_ge(t_hi_done, TRANS * p + n + 1)
                tiles = slice(h * QH, (h + 1) * QH)
                nc.vector.tensor_tensor(vv[:, tiles, :, HEAD:2 * HEAD],
                                        ps[:, TB[n % 2], :].rearrange("p (t n d) -> p t n d", t=QH, n=2),
                                        vv[:, tiles, :, 0:HEAD].bitcast(F32), ALU.subtract).then_inc(t_split, 1)

            def gate(p, h):
                dve.wait_ge(proj_hi_done, 6 * p + 4 + HALVES.index(h) + 1)
                half = silu[:, h * HALF:(h + 1) * HALF]
                nc.vector.tensor_tensor(half, ps[:, PROJ[h], :], half, ALU.mult).then_inc(bank_free[h], 1)

            def split_gated(n, s, first, end):
                dve.wait_ge(gs_hi_done, n + 1)
                hi, lo = (g[:, s % 2, first * P:end * P] for g in (gs_hi, gs_lo))
                nc.vector.tensor_tensor(lo.rearrange("p (e t) -> p e t", t=P), gated[:, first:end, s * P:(s + 1) * P],
                                        hi.bitcast(F32).rearrange("p (e t) -> p e t", t=P),
                                        ALU.subtract).then_inc(gs_split, 1)

            def split_wo(e):
                dve.wait_ge(wo_hi_done_act, e - POOL_WO + 1)
                nc.vector.tensor_tensor(wo_lo[:, e, :], w_raw[:, e % 2, :], wo_hi[:, e, :].bitcast(F32),
                                        ALU.subtract).then_inc(wo_split_dve, 1)

            def body(p, first=False, last=False):
                if not first:
                    for j in range(4):
                        wt_low(p - 1, 3, j)
                    sum_o(p - 1, 3)
                for s in range(4):
                    weights(p, s)
                    if s == 2:
                        v_low(p, 0)
                v_low(p, 1)
                for j in range(8):
                    wt_low(p, 0, j)
                    if j < 4:
                        weights(p, TILE0[1] + j)
                    if j == 3:
                        gate(p, 1)
                for j in range(4):
                    wt_low(p, 1, j)
                    if j == 0:
                        sum_o(p, 0)
                        gate(p, 0)
                    weights(p, TILE0[2] + j)
                    if last and j < 2:
                        split_gated(j, j, 0, PAIRS - 1)
                weights(p, TILE0[3])
                sum_o(p, 1)
                for j in range(8):
                    wt_low(p, 2, j)
                    if j < 3:
                        weights(p, TILE0[3] + 1 + j)
                    if last:
                        if j in (3, 5, 6):
                            split_wo((3, 5, 6).index(j) + POOL_WO)
                    elif j == 1:
                        split_qk(p + 1, K_, 1)
                    elif j == 3:
                        split_qk(p + 1, K_, 0)
                    elif j == 6:
                        split_qk(p + 1, Q_, 1)
                sum_o(p, 2)
                if not last:
                    split_qk(p + 1, Q_, 0)

            dve.wait_ge(w0_hi_done, 1)
            nc.vector.tensor_tensor(w_lo[:, 0, :], w_raw[:, K_, :], w_hi[:, 0, :].bitcast(F32),
                                    ALU.subtract).then_inc(w0_lo_done, 1)
            for k in range(KT):
                dve.wait_ge(x_hi_done, k + 1)
                nc.vector.tensor_tensor(x_lo[:, k, :], gated[:, k, :], x_hi[:, k, :].bitcast(F32),
                                        ALU.subtract).then_inc(x_lo_done, 1)
            for o in (K_, Q_):
                for h in HALVES:
                    split_qk(0, o, h)
            body(0, first=True)
            with dve.Fori(1, PAIRS - 1) as p:
                body(p)
            body(PAIRS - 1, last=True)
            for j in range(4):
                wt_low(PAIRS - 1, 3, j)
                if j == 1:
                    split_gated(2, 0, PAIRS - 1, PAIRS)
                    split_gated(3, 1, PAIRS - 1, PAIRS)
            sum_o(PAIRS - 1, 3)
            for s in range(ST):
                b = s % 2
                m = moments[:, b, :]
                mean, var, vare, rt, r0, t0 = (m[:, i:i + 1] for i in range(6))
                dve.wait_ge(y_done, s + 1)
                dve.wait_ge(res_loaded[b], 16 * (s // 2 + 1))
                if s == 0:
                    dve.wait_ge(lnp_loaded, 32)
                t = yt[b]
                nc.vector.scalar_tensor_tensor(
                    t.rearrange("p (n d) -> p n d", n=2), res[b].rearrange("p (n d) -> p n d", n=2), ALPHA,
                    ps[:, 2 * b:2 * b + 2, :], ALU.mult, ALU.add).then_inc(y_read, 1)
                if s + 2 < ST:
                    split_gated(s + 4, s + 2, 0, PAIRS)
                dve.wait_ge(y_read, s + 1)
                for h in range(2):
                    op = nc.vector.bn_stats(stats[:, b, h, :], t[:, h * HALF:(h + 1) * HALF])
                op.then_inc(scaled, 1)
                dve.wait_ge(scaled, 6 * s + 1)
                nc.vector.bn_aggr(m[:, 0:2], stats[:, b, :, :]).then_inc(ln_step, 1)
                dve.wait_ge(ln_step, 4 * s + 1)
                nc.vector.tensor_scalar(vare, var, EPS, None, ALU.add).then_inc(ln_step, 1)
                dve.wait_ge(root_done, s + 1)
                nc.vector.reciprocal(r0, rt).then_inc(ln_step, 1)
                dve.wait_ge(ln_step, 4 * s + 3)
                nc.vector.tensor_scalar(t0, vare, r0, r0, ALU.mult, ALU.mult).then_inc(scaled, 1)
                dve.wait_ge(scaled, 6 * s + 2)
                nc.vector.tensor_scalar(t0, t0, -0.5, 1.5, ALU.mult, ALU.add).then_inc(scaled, 1)
                dve.wait_ge(scaled, 6 * s + 3)
                nc.vector.tensor_tensor(r0, r0, t0, ALU.mult).then_inc(ln_step, 1)
                dve.wait_ge(ln_step, 4 * s + 4)
                nc.vector.tensor_scalar(t, t, mean, r0, ALU.subtract, ALU.mult).then_inc(scaled, 1)
                dve.wait_ge(scaled, 6 * s + 4)
                nc.vector.tensor_tensor(t, t, ln_par[:, 0, :], ALU.mult).then_inc(scaled, 1)
                dve.wait_ge(scaled, 6 * s + 5)
                nc.vector.tensor_tensor(res[b], t, ln_par[:, 1, :], ALU.add).then_inc(normed, 1)
                dve.wait_ge(normed, s + 1)
                nc.vector.tensor_copy(t0, t0).then_inc(scaled, 1)

        @block.gpsimd
        def _(pool):
            def split_w(p, o, gates=None):
                if gates is not None:
                    pool.wait_ge(gated_done, gates)
                pool.wait_ge(w_loaded[o % 2], 16 * (2 * p + o // 2 + 1))
                if not (isinstance(p, int) and p == 0 and o < 2):
                    pool.wait_ge(projected, 8 * p + 2 * o - 2)
                nc.gpsimd.tensor_tensor(w_hi[:, o % 2, :], w_raw[:, o % 2, :], ones[:, 0:1].broadcast_to([P, KT * P]),
                                        ALU.mult).then_inc(w_hi_done, 1)
                pool.wait_ge(w_hi_done, 4 * p + o)
                nc.gpsimd.tensor_tensor(w_lo[:, o % 2, :], w_raw[:, o % 2, :], w_hi[:, o % 2, :].bitcast(F32),
                                        ALU.subtract).then_inc(w_split, 1)

            def gate_o(p, unit, splits):
                head, half = UNITS[unit]
                pool.wait_ge(w_split, splits)
                if unit or not (isinstance(p, int) and p == 0):
                    pool.wait_ge(gated_done, 4 * p + unit)
                mine = slice(head * HEAD, (head + 1) * HEAD)
                cols = slice(half * HALF, (half + 1) * HALF)
                pool.wait_ge(o_summed, 4 * p + unit + 1)
                pool.wait_ge(bank_free[half], 4 * p + G_ + 1)
                nc.gpsimd.tensor_tensor(gated[mine, p, cols], osum[mine, half, :], silu[mine, cols],
                                        ALU.mult).then_inc(gated_done, 1)

            def split_wo(e):
                pool.wait_ge(w_loaded[e % 2], 16 * (2 * PAIRS + e // 2 + 1))
                nc.gpsimd.tensor_tensor(wo_hi[:, e, :], w_raw[:, e % 2, :], ones[:, 0:1].broadcast_to([P, DM]),
                                        ALU.mult).then_inc(wo_hi_done, 1)
                pool.wait_ge(wo_hi_done, e + 1)
                nc.gpsimd.tensor_tensor(wo_lo[:, e, :], w_raw[:, e % 2, :], wo_hi[:, e, :].bitcast(F32),
                                        ALU.subtract).then_inc(wo_split, 1)

            def body(p, first=False, last=False):
                split_w(p, G_, None if first else 4 * p - 1)
                if not first:
                    gate_o(p - 1, 3, 4 * p + 3)
                if not last:
                    split_w(p + 1, K_, None if first else 4 * p)
                gate_o(p, 0, 4 * p + (3 if last else 4))
                if not last:
                    split_w(p + 1, Q_, 4 * p + 1)
                else:
                    pool.wait_ge(projected, 8 * PAIRS)
                    pool.wait_ge(gated_done, 4 * p + 1)
                    for e in range(POOL_WO):
                        split_wo(e)
                    pool.wait_ge(wo_split, POOL_WO)
                gate_o(p, 1, 4 * p + (3 if last else 5))
                if not last:
                    split_w(p + 1, V_, 4 * p + 2)
                gate_o(p, 2, 4 * p + (3 if last else 6))

            nc.gpsimd.memset(ones[:, :], 1.0).then_inc(ones_set, 1)
            pool.wait_ge(ones_set, 1)
            split_w(0, Q_)
            split_w(0, V_)
            body(0, first=True)
            with pool.Fori(1, PAIRS - 1) as p:
                body(p)
            body(PAIRS - 1, last=True)

            gate_o(PAIRS - 1, 3, 4 * PAIRS - 1)


def kernel(x, w_in, w_out, ln_g, ln_b, rel_table):
    import concourse.bacc as bacc
    import ml_dtypes
    import numpy as np
    from concourse.bass_utils import run_bass_kernel_spmd

    x, w_in, w_out = np.asarray(x), np.asarray(w_in), np.asarray(w_out)
    rows = x[0, ::-1]
    w = w_in[0].reshape(KT, P, 4, PAIRS, P)[:, :, [1, 0, 2, 3]].transpose(3, 2, 1, 0, 4)
    one = np.eye(P, dtype=np.float32)
    not_past = np.where(np.arange(P)[None, :] <= np.arange(P)[:, None], np.float32(MASKED), np.float32(0))
    arrays = {
        "xT": rows.T.reshape(KT, P, SEQ),
        "x_rows": rows.reshape(ST, P, DM),
        "w_in": w.reshape(PAIRS, 4, P, KT * P),
        "w_out": w_out[0].reshape(PAIRS, P, DM),
        "ln_g": np.asarray(ln_g),
        "ln_b": np.asarray(ln_b),
        "consts_f": one,
        "consts_b": np.stack([one, not_past], axis=1).astype(ml_dtypes.bfloat16),
    }
    arrays = {f"in_{n}": np.ascontiguousarray(a) for n, a in arrays.items()}
    nc = bacc.Bacc("TRN2", target_bir_lowering=False, num_devices=1)
    args = [nc.dram_tensor(n, a.shape, mybir.dt.from_np(a.dtype), kind="ExternalInput").ap()
            for n, a in arrays.items()]
    args.append(nc.dram_tensor("out_y", (ST, P, DM), F32, kind="ExternalOutput").ap())
    stick_breaking_layer(nc, *args)
    r = run_bass_kernel_spmd(nc, [arrays], core_ids=[0])
    y = np.asarray(r.results[0]["out_y"])
    return y.reshape(1, SEQ, DM)[:, ::-1]
```

```python
from contextlib import ExitStack

import concourse.bass as bass
from concourse import mybir

F32 = mybir.dt.float32
F32R = mybir.dt.float32r
BF16 = mybir.dt.bfloat16
ALU = mybir.AluOpType
ACT = mybir.ActivationFunctionType

P = 128
SEQ = 1024
DM = 1024
HEAD = 64
PAIRS = 8
KT = DM // P
ST = SEQ // P
HALF = SEQ // 2
QH = ST // 2
SCALE = float(HEAD) ** -0.5
ALPHA = 2.0 ** 0.25
EPS = 1e-5

KEEPS = 4
POOL_WO = (2, 3, 4, 5)
FAST_WO = (0, 1, 6, 7)

K_, Q_, V_, G_ = range(4)
HALVES = (1, 0)

BEGIN, REST = slice(0, 2 * P), slice(2 * P, KT * P)

PROJ = (0, 1)
ZB = (2, 3, 4)
TB = (5, 6)
OB = 7

CHUNKS = 24
TILES = 16
STEPS = 24
TRANS = 2 + STEPS

UNITS = [(0, 0), (0, 1), (1, 0), (1, 1)]
CHUNK0 = [0, 8, 12, 20]
TILE0 = [0, 4, 8, 12]
STEP0 = [0, 8, 12, 20]

YB = (1, 0, 2, 3, 4, 5, 6)
EARLY = 3
STORES = {False: [slice(0, DM)], True: [slice(0, HALF), slice(HALF, 3 * DM // 4), slice(3 * DM // 4, DM)]}
BOTH = (0, 1)
FILL = [
    [((0, 0, (0,)), (0, 1, (0,))), ((0, 2, (0,)),), ((0, 3, (0,)), (0, 0, (1,))), ((0, 1, (1,)), (0, 2, (1,)))],
    [((0, 4, (0,)), (0, 3, (1,))), ((0, 4, (1,)),)],
    [((0, 5, (0,)),), ((0, 5, (1,)),), ((1, 0, BOTH),), ((1, 1, BOTH),), ((1, 2, BOTH),), ((0, 6, BOTH),),
     ((1, 3, BOTH),), ((1, 4, BOTH),)],
    [((1, 5, BOTH),), ((1, 6, BOTH), (2, 0, (0,))), ((2, 1, (0,)), (2, 2, (0,))),
     ((2, 3, (0,)), (2, 4, (0,)), (2, 5, (0,)))],
]


def chunks_of(tile):
    first = P * tile
    keys = SEQ - first
    if keys <= HALF:
        return [(first, keys)]
    size = min(HALF, keys - 2 * P)
    return [(first, size), (first + size, keys - size)]


def is_first(pair):
    return isinstance(pair, int) and pair == 0


CHUNK_LIST = [(u, half * QH + i, c) for u, (_, half) in enumerate(UNITS) for i in range(QH)
              for c in range(len(chunks_of(half * QH + i)))]


def w_offset(tile):
    half = tile // QH
    return sum(SEQ - P * t for t in range(half * QH, tile))


W_SIZE = [w_offset(QH - 1) + SEQ - P * (QH - 1), w_offset(ST - 1) + SEQ - P * (ST - 1)]


def key_tiles(unit):
    return list(range(ST - 1, UNITS[unit][1] * QH - 1, -1))


def stick_breaking_layer(nc, xT, x_rows, w_in, w_out, ln_g, ln_b, consts_f, consts_b, out):
    with ExitStack() as ctx:
        def sb(name, shape, dt=F32):
            return ctx.enter_context(nc.sbuf_tensor(name, shape, dt))

        def sem(name):
            return ctx.enter_context(nc.semaphore(name))

        ps = ctx.enter_context(nc.psum_tensor("ps", [P, 8, HALF], F32))

        x_hi = sb("x_hi", [P, KT, SEQ], F32R)
        x_lo = sb("x_lo", [P, KT, SEQ], F32R)
        w_raw = sb("w_raw", [P, 2, KT * P])
        wo_raw = sb("wo_raw", [P, 2, DM])
        w_hi = sb("w_hi", [P, 2, KT * P], F32R)
        w_lo = sb("w_lo", [P, 2, KT * P], F32R)
        kk = sb("kk", [P, 4, SEQ], F32R)
        qq = sb("qq", [P, 2, SEQ], F32R)
        vT = sb("vT", [P, SEQ])
        vv = sb("vv", [P, ST, 2, 2 * HEAD], F32R)
        gated = sb("gated", [P, PAIRS, SEQ])
        silu = sb("silu", [P, SEQ])
        take = [sb(f"take{h}", [P, W_SIZE[h]]) for h in range(2)]
        keep = sb("keep", [P, KEEPS, 1 + SEQ])
        wt_hi = sb("wt_hi", [P, 2, HALF], F32R)
        wt_lo = sb("wt_lo", [P, 2, HALF], F32R)
        osum = sb("osum", [P, 2, HALF])
        ident = sb("ident", [P, P])
        first_key = sb("first_key", [P, SEQ], BF16)
        ones = sb("ones", [P, 1])
        stats = sb("stats", [P, 2, 2, 6])
        moments = sb("moments", [P, 2, 8])

        x0_loaded = [sem("x0_loaded0"), sem("x0_loaded1")]
        x_loaded = [None] + [sem(f"x_loaded{k}") for k in range(1, KT)]
        consts_loaded = sem("consts_loaded")
        w_loaded = [sem("w_loaded0"), sem("w_loaded1")]
        wo_loaded = [sem("wo_loaded0"), sem("wo_loaded1")]
        k_copied = sem("k_copied")
        ones_set = sem("ones_set")
        zero_set = sem("zero_set")
        x_hi_done = sem("x_hi_done")
        x_lo_done = sem("x_lo_done")
        begin_loaded = [sem("begin_loaded_k"), sem("begin_loaded_q")]
        k0_hi_done = sem("k0_hi_done")
        k0_split = sem("k0_split")
        q0_hi_done = sem("q0_hi_done")
        q0_split = sem("q0_split")
        w_hi_done = sem("w_hi_done")
        w_split = sem("w_split")
        projected = sem("projected")
        proj_hi_done = sem("proj_hi_done")
        bank_free = [sem("bank_free0"), sem("bank_free1")]
        z_done = sem("z_done")
        sigmoids_done = sem("sigmoids_done")
        scanned = sem("scanned")
        w_ready = sem("w_ready")
        transposed = sem("transposed")
        t_hi_done = sem("t_hi_done")
        t_split = sem("t_split")
        stepped = sem("stepped")
        o_moved = sem("o_moved")
        o_summed = sem("o_summed")
        gated_done = sem("gated_done")
        x_used = sem("x_used")
        wo_hi_done = sem("wo_hi_done")
        wo_split = sem("wo_split")
        wo_hi_done_act = sem("wo_hi_done_act")
        wo_split_dve = sem("wo_split_dve")
        gs_hi_done = sem("gs_hi_done")
        gs_split = sem("gs_split")
        lnp_loaded = sem("lnp_loaded")
        res_loaded = [sem("res_loaded0"), sem("res_loaded1")]
        y_done = sem("y_done")
        var_ready = sem("var_ready")
        root_done = sem("root_done")
        y_read = sem("y_read")
        chained = sem("chained")
        normed = sem("normed")
        stored = [sem("stored0"), sem("stored1")]

        wo_hi, wo_lo = x_hi, x_lo
        gs = [(w_hi[:, 0, :], w_lo[:, 0, :]), (w_hi[:, 1, :], w_lo[:, 1, :]), (kk[:, 0, :], kk[:, 1, :]),
              (kk[:, 2, :], kk[:, 3, :])]
        ln_par = keep
        take0 = take[0][:, 0:2 * DM].rearrange("p (n d) -> p n d", n=2)
        res = [take0[:, 0, :], take0[:, 1, :]]
        yt = [keep[:, 2, 0:DM], keep[:, 3, 0:DM]]

        def x_parts(k):
            if k:
                return [(slice(0, SEQ), x_loaded[k])]
            return [(slice(h * HALF, (h + 1) * HALF), x0_loaded[h]) for h in HALVES]

        block = ctx.enter_context(nc.Block())

        @block.sync
        def _(sp):
            def load_w(p, o):
                sp.dma_start(w_raw[:, o % 2, :], w_in[p, o]).then_inc(w_loaded[o % 2], 16)

            def load_w0(o, part, signal):
                sp.dma_start(w_raw[:, o, part], w_in[0, o, :, part]).then_inc(signal, 16)

            load_w0(K_, BEGIN, begin_loaded[K_])
            for k in range(KT):
                if k == 0:
                    for h in HALVES:
                        cols = slice(h * HALF, (h + 1) * HALF)
                        sp.dma_start(gated[:, 0, cols], xT[0, :, cols]).then_inc(x0_loaded[h], 16)
                    load_w0(Q_, BEGIN, begin_loaded[Q_])
                else:
                    sp.dma_start(gated[:, k, :], xT[k]).then_inc(x_loaded[k], 16)
                if k == 1:
                    load_w0(K_, REST, w_loaded[K_])
                    load_w0(Q_, REST, w_loaded[Q_])
            sp.dma_start(ident[:, :], consts_f).then_inc(consts_loaded, 16)
            sp.dma_start(first_key[:, :], consts_b).then_inc(consts_loaded, 16)
            sp.wait_ge(k0_split, 2)
            load_w(0, V_)
            sp.wait_ge(w_split, 1)
            load_w(0, G_)

            def duplicate_k(p):
                for h in range(2):
                    sp.wait_ge(bank_free[h], 4 * p + K_ + 1)
                sp.dma_start(kk[HEAD:P, 0:2, :].bitcast(F32), kk[0:HEAD, 0:2, :].bitcast(F32)).then_inc(k_copied, 16)
                sp.dma_start(kk[0:HEAD, 2:4, :].bitcast(F32), kk[HEAD:P, 2:4, :].bitcast(F32)).then_inc(k_copied, 16)

            def body(p):
                for o in (K_, Q_, V_, G_):
                    sp.wait_ge(w_split, 4 * p + o + 2)
                    load_w(p + 1, o)
                duplicate_k(p + 1)

            duplicate_k(0)
            body(0)
            with sp.Fori(1, PAIRS - 1) as p:
                body(p)

            for i in range(2):
                sp.dma_start(wo_raw[:, i, :], w_out[FAST_WO[i]]).then_inc(wo_loaded[i], 16)
            for i, e in enumerate(POOL_WO):
                if i < 2:
                    sp.wait_ge(w_split, 4 * PAIRS - 2 + i)
                else:
                    sp.wait_ge(wo_split, i - 1)
                sp.dma_start(w_raw[:, i % 2, :], w_out[e]).then_inc(w_loaded[i % 2], 16)
                if i in (1, 2):
                    sp.wait_ge(wo_split_dve, i)
                    sp.dma_start(wo_raw[:, i - 1, :], w_out[FAST_WO[i + 1]]).then_inc(wo_loaded[i - 1], 16)
            sp.wait_ge(w_ready, TILES * PAIRS)
            sp.dma_start(ln_par[:, 0, 0:DM], ln_g.broadcast_to([P, DM])).then_inc(lnp_loaded, 16)
            sp.dma_start(ln_par[:, 1, 0:DM], ln_b.broadcast_to([P, DM])).then_inc(lnp_loaded, 16)
            sp.wait_ge(transposed, TRANS * (PAIRS - 1) + 2 + STEP0[3])
            for s in range(2):
                sp.dma_start(res[s], x_rows[s]).then_inc(res_loaded[s], 16)
            for s in range(ST):
                for n, cols in enumerate(STORES[s == ST - 1]):
                    sp.wait_ge(normed, s + n + 1)
                    sp.dma_start(out[s, :, cols], res[s % 2][:, cols]).then_inc(stored[s % 2], 16)
                if s + 2 < ST:
                    sp.wait_ge(stored[s % 2], 16 * (s // 2 + 1))
                    sp.dma_start(res[s % 2], x_rows[s + 2]).then_inc(res_loaded[s % 2], 16)
            sp.wait_ge(stored[0], 16 * (ST // 2))
            sp.wait_ge(stored[1], 16 * (ST // 2 - 1 + len(STORES[True])))

        @block.tensor
        def _(pe):
            def project(p, o, first, count, last=False):
                for m in range(first, first + count):
                    n, k, part = m // (3 * KT), m // 3 % KT, m % 3
                    h = HALVES[n]
                    if m == 0:
                        pe.wait_ge(w_split, 4 * p + o)
                    if m % (3 * KT) == 0:
                        pe.wait_ge(bank_free[h], K_ + 1 if o == V_ and is_first(p) else 4 * p + o)
                    mm = project_part(o, h, k, part, PROJ[h])
                    if o == G_ and last and n == 1 and part == 2 and k < KT - 1:
                        mm.then_inc(x_used, 1)

            def project_part(o, h, k, part, bank):
                w = (w_hi, w_hi, w_lo)[part][:, o % 2, k * P:(k + 1) * P]
                x = (x_hi, x_lo, x_hi)[part][:, k, h * HALF:(h + 1) * HALF]
                last = k == KT - 1 and part == 2
                mm = nc.tensor.matmul(ps[:, bank, :], w, x, start=(k == 0 and part == 0), stop=last)
                if last:
                    mm.then_inc(projected, 1)
                return mm

            def scores(p, n):
                unit, tile, c = CHUNK_LIST[n]
                head = UNITS[unit][0]
                key, keys = chunks_of(tile)[c]
                if n in (0, CHUNK0[2]):
                    pe.wait_ge(k_copied, 32 * (p + 1))
                    for h in range(2):
                        pe.wait_ge(bank_free[h], 4 * p + Q_ + 1)
                if n >= len(ZB) or not is_first(p):
                    pe.wait_ge(sigmoids_done, CHUNKS * p + n - len(ZB) + 1)
                z = ps[:, ZB[n % len(ZB)], 0:keys]
                q = qq[:, head, tile * P:(tile + 1) * P]
                nc.tensor.matmul(z, q, kk[:, 2 * head, key:key + keys], start=True, stop=False)
                nc.tensor.matmul(z, q, kk[:, 2 * head + 1, key:key + keys], start=False,
                                 stop=True).then_inc(z_done, 1)

            def transpose_v(p, n):
                h = HALVES[n]
                pe.wait_ge(bank_free[h], 4 * p + V_ + 1)
                if not is_first(p):
                    pe.wait_ge(t_split, TRANS * p + n - 1)
                for i in range(QH):
                    t = h * QH + i
                    mm = nc.tensor.transpose(ps[:, TB[n % 2], i * P:(i + 1) * P], vT[:, t * P:(t + 1) * P],
                                             ident[:, :])
                mm.then_inc(transposed, 1)

            def transpose_w(p, unit, j):
                head, half = UNITS[unit]
                tile = key_tiles(unit)[j]
                if j == 0:
                    pe.wait_ge(w_ready, TILES * p + TILE0[unit] + QH)
                n = STEP0[unit] + j
                pe.wait_ge(t_split, TRANS * p + 2 + n - 1)
                for i in range(min(tile - half * QH + 1, QH)):
                    q = half * QH + i
                    at = w_offset(q) + (tile - q) * P
                    mm = nc.tensor.transpose(ps[:, TB[n % 2], i * P:(i + 1) * P], take[half][:, at:at + P],
                                             ident[:, :])
                mm.then_inc(transposed, 1)

            def values(p, unit, j):
                head, half = UNITS[unit]
                tile = key_tiles(unit)[j]
                n = STEP0[unit] + j
                pe.wait_ge(t_split, TRANS * p + 2 + n + 1)
                if j == 0 and not (unit == 0 and is_first(p)):
                    pe.wait_ge(o_summed, 4 * p + unit)
                cols = min(tile - half * QH + 1, QH) * P
                last = j == len(key_tiles(unit)) - 1
                nc.tensor.matmul(ps[:, OB, 0:cols], vv[:, tile, head, :], wt_hi[:, n % 2, 0:cols],
                                 start=(j == 0), stop=False)
                nc.tensor.matmul(ps[:, OB, 0:cols], vv[:, tile, head, :], wt_lo[:, n % 2, 0:cols],
                                 start=False, stop=last).then_inc(stepped, 1)

            def output(s, e, halves=BOTH):
                if s < EARLY and e == 0:
                    pe.wait_ge(gs_split, s + 1)
                elif e == (PAIRS - 1 if s < EARLY else 0):
                    pe.wait_ge(gs_split, EARLY + s + 1)
                if s == 0:
                    if e in POOL_WO:
                        pe.wait_ge(wo_split, POOL_WO.index(e) + 1)
                    else:
                        pe.wait_ge(wo_split_dve, FAST_WO.index(e) + 1)
                for h in halves:
                    n = 2 * s + h
                    bank = YB[n % len(YB)]
                    if e == 0:
                        if n >= len(YB):
                            pe.wait_ge(y_read, n - len(YB) + 1)
                        elif bank in PROJ:
                            pe.wait_ge(bank_free[bank], 4 * PAIRS)
                        elif bank in ZB:
                            pe.wait_ge(sigmoids_done, CHUNKS * PAIRS - (1 if bank < ZB[2] else 0))
                        else:
                            pe.wait_ge(t_split, TRANS * PAIRS)
                    for part in range(3):
                        a = gs[s % 4][part // 2][:, e * P:(e + 1) * P]
                        b = (wo_hi, wo_lo, wo_hi)[part][:, e, h * HALF:(h + 1) * HALF]
                        mm = nc.tensor.matmul(ps[:, bank, :], a, b, start=(e == 0 and part == 0),
                                              stop=(e == PAIRS - 1 and part == 2))
                    if e == PAIRS - 1:
                        mm.then_inc(y_done, 1)

            def fill(parts):
                for s, e, halves in parts:
                    output(s, e, halves)

            def last_unit(p, between):
                for j in range(4):
                    transpose_w(p, 3, j)
                    between(j)
                    if j:
                        values(p, 3, j - 1)
                values(p, 3, 3)

            def body(p, first=False, last=False):
                if first:
                    project(p, V_, 0, 30)
                else:
                    last_unit(p - 1, lambda j: project(p, V_, (0, 8, 16, 23)[j], (8, 8, 7, 7)[j]))
                at = 30
                for n, count in enumerate((2, 2, 2, 2, 2, 2, 4, 2)):
                    scores(p, n)
                    project(p, V_, at, count)
                    at += count
                    if n == 3:
                        transpose_v(p, 0)
                project(p, G_, 0, 12, last)
                transpose_v(p, 1)
                scores(p, CHUNK0[1])
                project(p, G_, 12, 8, last)
                for j in range(8):
                    transpose_w(p, 0, j)
                    if 0 < j < 4:
                        scores(p, CHUNK0[1] + j)
                    project(p, G_, 20 + 7 * j // 2, 7 * (j + 1) // 2 - 7 * j // 2, last)
                    if j == 7:
                        scores(p, CHUNK0[2])
                    if j:
                        values(p, 0, j - 1)
                for j in range(4):
                    transpose_w(p, 1, j)
                    scores(p, CHUNK0[2] + 2 * j + 1)
                    if not last:
                        project(p + 1, K_, 5 * j, 2)
                    if j == 0:
                        values(p, 0, 7)
                    scores(p, CHUNK0[2] + 2 * j + 2)
                    if not last:
                        project(p + 1, K_, 5 * j + 2, 3)
                    else:
                        fill(FILL[0][j])
                    if j:
                        values(p, 1, j - 1)
                for c in range(2):
                    if c == 1:
                        scores(p, CHUNK0[3] + 1)
                    if not last:
                        project(p + 1, K_, 20 + 5 * c, 5 + 4 * c)
                    else:
                        fill(FILL[1][c])
                    if c == 1:
                        values(p, 1, 3)
                for j in range(8):
                    transpose_w(p, 2, j)
                    if j < 2:
                        scores(p, CHUNK0[3] + 2 + j)
                    if last:
                        fill(FILL[2][j])
                    elif j < 3:
                        project(p + 1, K_, (34, 38, 43)[j], (4, 5, 5)[j])
                    else:
                        project(p + 1, Q_, 10 * (j - 3), 10 if j < 7 else 8)
                    if j:
                        values(p, 2, j - 1)
                values(p, 2, 7)

            order = ((K_, 0), (Q_, 0), (K_, 1), (Q_, 1), (K_, 2), (K_, 3), (Q_, 2), (K_, 4), (Q_, 3), (K_, 5),
                     (Q_, 4), (K_, 6), (K_, 7), (Q_, 5), (Q_, 6), (Q_, 7))
            for o, k in order:
                for h in HALVES:
                    for part in range(3):
                        if o == K_ and (h == HALVES[0] or k == 0):
                            count = 1 + HALVES.index(h) if k == 0 else k + 2
                            if part == 0:
                                pe.wait_ge(x_hi_done, count)
                            if part == 1:
                                pe.wait_ge(x_lo_done, count)
                        if h == HALVES[0]:
                            if o == K_ and part == 0 and k in (0, 2):
                                pe.wait_ge(k0_hi_done, k // 2 + 1)
                            if o == K_ and part == 2 and k in (0, 2):
                                pe.wait_ge(k0_split, k // 2 + 1)
                            if o == Q_ and part == 0 and k == 0:
                                pe.wait_ge(q0_split, 1)
                            if o == Q_ and part == 0 and k == 2:
                                pe.wait_ge(w_split, Q_)
                        project_part(o, h, k, part, PROJ[h] if o == K_ else ZB[h])
            pe.wait_ge(consts_loaded, 32)
            body(0, first=True)
            with pe.Fori(1, PAIRS - 1) as p:
                body(p)
            body(PAIRS - 1, last=True)
            last_unit(PAIRS - 1, lambda j: fill(FILL[3][j]))

            done = {(s, e, h) for group in FILL for parts in group for s, e, halves in parts for h in halves}
            for s in range(ST):
                for h in range(2):
                    fill([(s, e, (h,)) for e in range(PAIRS) if (s, e, h) not in done])

        @block.scalar
        def _(act):
            def copy(dst, src):
                return nc.scalar.activation(dst, src, ACT.Copy)

            def sigmoids(p, n):
                unit, tile, c = CHUNK_LIST[n]
                half = UNITS[unit][1]
                key, keys = chunks_of(tile)[c]
                number = TILE0[unit] + tile - half * QH
                act.wait_ge(z_done, CHUNKS * p + n + 1)
                if c == 0 and (number >= KEEPS or not is_first(p)):
                    act.wait_ge(w_ready, TILES * p + number - KEEPS + 1)
                if n == CHUNK0[unit] and (unit >= 2 or not is_first(p)):
                    before = STEP0[unit - 1] if unit >= 2 else STEP0[unit + 2] + (8, 4)[half] - TRANS
                    act.wait_ge(transposed, TRANS * p + 2 + before)
                z = ps[:, ZB[n % len(ZB)], 0:keys]
                off = key - P * tile
                nc.scalar.activation(keep[:, number % KEEPS, 1 + off:1 + off + keys], z, ACT.Sigmoid, scale=-SCALE)
                at = w_offset(tile) + off
                nc.scalar.activation(take[half][:, at:at + keys], z, ACT.Sigmoid,
                                     scale=SCALE).then_inc(sigmoids_done, 1)

            def wt_high(p, unit, j):
                n = STEP0[unit] + j
                cols = min(key_tiles(unit)[j] - UNITS[unit][1] * QH + 1, QH) * P
                act.wait_ge(transposed, TRANS * p + 2 + n + 1)
                if n >= 2 or not is_first(p):
                    act.wait_ge(stepped, STEPS * p + n - 1)
                copy(wt_hi[:, n % 2, 0:cols], ps[:, TB[n % 2], 0:cols]).then_inc(t_hi_done, 1)

            def move_o(p, unit):
                head, half = UNITS[unit]
                act.wait_ge(stepped, STEPS * p + STEP0[unit] + len(key_tiles(unit)))
                if not is_first(p):
                    act.wait_ge(gated_done, 4 * (p - 1) + unit + 1)
                mine = slice(head * HEAD, (head + 1) * HEAD)
                other = slice((1 - head) * HEAD, (2 - head) * HEAD)
                copy(osum[mine, half, :], ps[other, OB, :]).then_inc(o_moved, 1)

            def split_qk(p, o, h):
                cols = slice(h * HALF, (h + 1) * HALF)
                act.wait_ge(projected, 8 * p + 2 * o + HALVES.index(h) + 1)
                if not is_first(p):
                    act.wait_ge(z_done, CHUNKS * p)
                a = kk[0:HEAD, 0, cols] if o == K_ else qq[0:HEAD, 0, cols]
                b = kk[HEAD:P, 2, cols] if o == K_ else qq[HEAD:P, 1, cols]
                bank = ZB[h] if o == Q_ and is_first(p) else PROJ[h]
                copy(a, ps[0:HEAD, bank, :])
                copy(b, ps[HEAD:P, bank, :]).then_inc(proj_hi_done, 1)

            def copy_v(p, h):
                act.wait_ge(projected, 8 * p + 2 * V_ + HALVES.index(h) + 1)
                if is_first(p):
                    act.wait_ge(bank_free[h], Q_ + 1)
                copy(vT[:, h * HALF:(h + 1) * HALF], ps[:, PROJ[h], :]).then_inc(bank_free[h], 1)

            def v_high(p, n):
                h = HALVES[n]
                act.wait_ge(transposed, TRANS * p + n + 1)
                if n == 0 and not is_first(p):
                    act.wait_ge(stepped, STEPS * p)
                copy(vv[:, h * QH:(h + 1) * QH, :, 0:HEAD],
                     ps[:, TB[n % 2], :].rearrange("p (t n d) -> p t n d", t=QH, n=2)).then_inc(t_hi_done, 1)

            def gate_sigmoid(p, h):
                act.wait_ge(projected, 8 * p + 2 * G_ + HALVES.index(h) + 1)
                if h == HALVES[0] and not is_first(p):
                    act.wait_ge(gated_done, 4 * p)
                nc.scalar.activation(silu[:, h * HALF:(h + 1) * HALF], ps[:, PROJ[h], :],
                                     ACT.Sigmoid).then_inc(proj_hi_done, 1)

            def split_gated(s, first, end):
                if end < PAIRS:
                    act.wait_ge(gated_done, 4 * end)
                else:
                    act.wait_ge(gated_done, 4 * PAIRS - (1 if s < QH else 0))
                if s >= 4:
                    act.wait_ge(y_done, 2 * (s - 3))
                elif s >= 2:
                    act.wait_ge(z_done, CHUNKS * PAIRS)
                else:
                    act.wait_ge(projected, 8 * PAIRS - 2 + 2 * s)
                copy(gs[s % 4][0][:, first * P:end * P].rearrange("p (e t) -> p e t", t=P),
                     gated[:, first:end, s * P:(s + 1) * P]).then_inc(gs_hi_done, 1)

            def split_wo(i):
                e = FAST_WO[i]
                act.wait_ge(wo_loaded[i % 2], 16 * (i // 2 + 1))
                if e < KT - 1:
                    act.wait_ge(x_used, e + 1)
                else:
                    act.wait_ge(projected, 8 * PAIRS)
                copy(wo_hi[:, e, :], wo_raw[:, i % 2, :]).then_inc(wo_hi_done_act, 1)

            def body(p, first=False, last=False):
                if not first:
                    for j in range(4):
                        wt_high(p - 1, 3, j)
                    move_o(p - 1, 3)
                copy_v(p, 1)
                for s in range(4):
                    if s == 2:
                        v_high(p, 0)
                    sigmoids(p, 2 * s)
                    sigmoids(p, 2 * s + 1)
                copy_v(p, 0)
                v_high(p, 1)
                sigmoids(p, CHUNK0[1])
                for j in range(8):
                    wt_high(p, 0, j)
                    if 0 < j < 4:
                        sigmoids(p, CHUNK0[1] + j)
                    if j == 3:
                        gate_sigmoid(p, 1)
                    if last and j == 4:
                        split_gated(0, 0, PAIRS - 1)
                    if last and j in (5, 6):
                        split_wo(j - 5)
                sigmoids(p, CHUNK0[2])
                for j in range(4):
                    wt_high(p, 1, j)
                    for c in (1, 2):
                        sigmoids(p, CHUNK0[2] + 2 * j + c)
                        if j == 0 and c == 1:
                            move_o(p, 0)
                    if j == (0 if last else 1):
                        gate_sigmoid(p, 0)
                sigmoids(p, CHUNK0[3] + 1)
                if last:
                    split_gated(1, 0, PAIRS - 1)
                move_o(p, 1)
                for j in range(8):
                    wt_high(p, 2, j)
                    if j < 2:
                        sigmoids(p, CHUNK0[3] + 2 + j)
                    if last:
                        if j == 4:
                            split_gated(2, 0, PAIRS - 1)
                        if j in (2, 3):
                            split_wo(j)
                    elif j == 1:
                        split_qk(p + 1, K_, 1)
                    elif j == 3:
                        split_qk(p + 1, K_, 0)
                    elif j == 6:
                        split_qk(p + 1, Q_, 1)
                move_o(p, 2)
                if not last:
                    split_qk(p + 1, Q_, 0)

            act.wait_ge(begin_loaded[K_], 16)
            copy(w_hi[:, K_, BEGIN], w_raw[:, K_, BEGIN]).then_inc(k0_hi_done, 1)
            for k in range(KT):
                for cols, signal in x_parts(k):
                    act.wait_ge(signal, 16)
                    copy(x_hi[:, k, cols], gated[:, k, cols]).then_inc(x_hi_done, 1)
                if k == 1:
                    act.wait_ge(w_loaded[K_], 16)
                    copy(w_hi[:, K_, REST], w_raw[:, K_, REST]).then_inc(k0_hi_done, 1)
            act.wait_ge(w_loaded[0], 32)
            act.wait_ge(projected, 2)
            act.wait_ge(w_split, Q_)
            copy(w_hi[:, 0, :], w_raw[:, 0, :]).then_inc(w_hi_done, 1)
            for o in (K_, Q_):
                for h in HALVES:
                    split_qk(0, o, h)
            body(0, first=True)
            with act.Fori(1, PAIRS - 1) as p:
                body(p)
            body(PAIRS - 1, last=True)
            for j in range(4):
                wt_high(PAIRS - 1, 3, j)
                if j == 1:
                    for s in range(EARLY):
                        split_gated(s, PAIRS - 1, PAIRS)
            split_gated(EARLY, 0, PAIRS)
            move_o(PAIRS - 1, 3)
            for s in range(ST):
                if s + 4 < ST:
                    split_gated(s + 4, 0, PAIRS)
                act.wait_ge(var_ready, s + 1)
                nc.scalar.activation(moments[:, s % 2, 3:4], moments[:, s % 2, 2:3], ACT.Sqrt).then_inc(root_done, 1)

        @block.vector
        def _(dve):
            def weights(p, number, between=None):
                unit = number // QH
                half = UNITS[unit][1]
                tile = half * QH + number % QH
                keys = SEQ - P * tile
                last_chunk = max(n for n, (u, t, _) in enumerate(CHUNK_LIST) if u == unit and t == tile)
                dve.wait_ge(sigmoids_done, CHUNKS * p + last_chunk + 1)
                kept = keep[:, number % KEEPS, 0:keys]
                nc.vector.tensor_tensor_scan(kept, kept, first_key[:, 0:keys], 0.0, ALU.mult,
                                             ALU.max).then_inc(scanned, 1)
                if between:
                    between()
                at = w_offset(tile)
                dve.wait_ge(scanned, TILES * p + number + 1)
                w = take[half][:, at:at + keys]
                nc.vector.tensor_tensor(w, w, kept, ALU.mult).then_inc(w_ready, 1)

            def wt_low(p, unit, j):
                n = STEP0[unit] + j
                cols = min(key_tiles(unit)[j] - UNITS[unit][1] * QH + 1, QH) * P
                dve.wait_ge(t_hi_done, TRANS * p + 2 + n + 1)
                nc.vector.tensor_tensor(wt_lo[:, n % 2, 0:cols], ps[:, TB[n % 2], 0:cols],
                                        wt_hi[:, n % 2, 0:cols].bitcast(F32), ALU.subtract).then_inc(t_split, 1)

            def sum_o(p, unit):
                head, half = UNITS[unit]
                mine = slice(head * HEAD, (head + 1) * HEAD)
                dve.wait_ge(o_moved, 4 * p + unit + 1)
                nc.vector.tensor_tensor(osum[mine, half, :], ps[mine, OB, :], osum[mine, half, :],
                                        ALU.add).then_inc(o_summed, 1)

            def split_qk(p, o, h):
                cols = slice(h * HALF, (h + 1) * HALF)
                dve.wait_ge(proj_hi_done, 6 * p + 2 * o + HALVES.index(h) + 1)
                if o == K_:
                    parts = [(kk[0:HEAD, 1, cols], kk[0:HEAD, 0, cols], 0),
                             (kk[HEAD:P, 3, cols], kk[HEAD:P, 2, cols], 1)]
                else:
                    parts = [(qq[HEAD:P, 0, cols], qq[0:HEAD, 0, cols], 0),
                             (qq[0:HEAD, 1, cols], qq[HEAD:P, 1, cols], 1)]
                bank = ZB[h] if o == Q_ and is_first(p) else PROJ[h]
                for lo, hi, head in parts:
                    op = nc.vector.tensor_tensor(lo, ps[head * HEAD:(head + 1) * HEAD, bank, :],
                                                 hi.bitcast(F32), ALU.subtract)
                op.then_inc(bank_free[h], 1)

            def v_low(p, n):
                h = HALVES[n]
                dve.wait_ge(t_hi_done, TRANS * p + n + 1)
                tiles = slice(h * QH, (h + 1) * QH)
                nc.vector.tensor_tensor(vv[:, tiles, :, HEAD:2 * HEAD],
                                        ps[:, TB[n % 2], :].rearrange("p (t n d) -> p t n d", t=QH, n=2),
                                        vv[:, tiles, :, 0:HEAD].bitcast(F32), ALU.subtract).then_inc(t_split, 1)

            def gate(p, h):
                dve.wait_ge(proj_hi_done, 6 * p + 4 + HALVES.index(h) + 1)
                half = silu[:, h * HALF:(h + 1) * HALF]
                nc.vector.tensor_tensor(half, ps[:, PROJ[h], :], half, ALU.mult).then_inc(bank_free[h], 1)

            def split_gated(n, s, first, end):
                dve.wait_ge(gs_hi_done, n + 1)
                hi, lo = (g[:, first * P:end * P] for g in gs[s % 4])
                nc.vector.tensor_tensor(lo.rearrange("p (e t) -> p e t", t=P), gated[:, first:end, s * P:(s + 1) * P],
                                        hi.bitcast(F32).rearrange("p (e t) -> p e t", t=P),
                                        ALU.subtract).then_inc(gs_split, 1)

            def split_wo(i):
                e = FAST_WO[i]
                dve.wait_ge(wo_hi_done_act, i + 1)
                nc.vector.tensor_tensor(wo_lo[:, e, :], wo_raw[:, i % 2, :], wo_hi[:, e, :].bitcast(F32),
                                        ALU.subtract).then_inc(wo_split_dve, 1)

            def body(p, first=False, last=False):
                if not first:
                    for j in range(4):
                        wt_low(p - 1, 3, j)
                    sum_o(p - 1, 3)
                for s in range(4):
                    if s == 2:
                        v_low(p, 0)
                    weights(p, s)
                v_low(p, 1)
                for j in range(8):
                    wt_low(p, 0, j)
                    if j < 4:
                        weights(p, TILE0[1] + j)
                    if j == 3:
                        gate(p, 1)
                    if last and j == 4:
                        split_gated(0, 0, 0, PAIRS - 1)
                    if last and j in (5, 6):
                        split_wo(j - 5)
                for j in range(4):
                    wt_low(p, 1, j)
                    if j == (1 if last else 2):
                        gate(p, 0)
                    weights(p, TILE0[2] + j, (lambda: sum_o(p, 0)) if j == 0 else None)
                weights(p, TILE0[3])
                sum_o(p, 1)
                for j in range(8):
                    wt_low(p, 2, j)
                    if last and j == 0:
                        split_gated(1, 1, 0, PAIRS - 1)
                    if last:
                        if j == 4:
                            split_gated(2, 2, 0, PAIRS - 1)
                        if j in (2, 3):
                            split_wo(j)
                    elif j == 1:
                        split_qk(p + 1, K_, 1)
                    elif j == 3:
                        split_qk(p + 1, K_, 0)
                    elif j == 6:
                        split_qk(p + 1, Q_, 1)
                    if j < 3:
                        weights(p, TILE0[3] + 1 + j)
                sum_o(p, 2)
                if not last:
                    split_qk(p + 1, Q_, 0)

            nc.vector.memset(keep[:, :, 0:1], 0.0).then_inc(zero_set, 1)
            def split_k0(n, part):
                dve.wait_ge(k0_hi_done, n + 1)
                nc.vector.tensor_tensor(w_lo[:, K_, part], w_raw[:, K_, part], w_hi[:, K_, part].bitcast(F32),
                                        ALU.subtract).then_inc(k0_split, 1)

            split_k0(0, BEGIN)
            for k in range(KT):
                for n, (cols, _) in enumerate(x_parts(k)):
                    dve.wait_ge(x_hi_done, 1 + n if k == 0 else k + 2)
                    nc.vector.tensor_tensor(x_lo[:, k, cols], gated[:, k, cols], x_hi[:, k, cols].bitcast(F32),
                                            ALU.subtract).then_inc(x_lo_done, 1)
                if k == 1:
                    split_k0(1, REST)
            dve.wait_ge(w_hi_done, V_)
            nc.vector.tensor_tensor(w_lo[:, 0, :], w_raw[:, 0, :], w_hi[:, 0, :].bitcast(F32),
                                    ALU.subtract).then_inc(w_split, 1)
            for o in (K_, Q_):
                for h in HALVES:
                    split_qk(0, o, h)
            dve.wait_ge(consts_loaded, 32)
            dve.wait_ge(zero_set, 1)
            body(0, first=True)
            with dve.Fori(1, PAIRS - 1) as p:
                body(p)
            body(PAIRS - 1, last=True)
            for j in range(4):
                wt_low(PAIRS - 1, 3, j)
                if j == 1:
                    for s in range(EARLY):
                        split_gated(EARLY + s, s, PAIRS - 1, PAIRS)
            split_gated(2 * EARLY, EARLY, 0, PAIRS)
            sum_o(PAIRS - 1, 3)
            steps = [0]

            def chain(op, between=None):
                steps[0] += 1
                op.then_inc(chained, 1)
                if between:
                    between()
                dve.wait_ge(chained, steps[0])

            for s in range(ST):
                b = s % 2
                m = moments[:, b, :]
                mean, var, var_eps, sd, r, c = (m[:, i:i + 1] for i in range(6))
                t = yt[b]
                dve.wait_ge(res_loaded[b], 16 * (s // 2 + 1))
                for h in range(2):
                    cols = slice(h * HALF, (h + 1) * HALF)
                    dve.wait_ge(y_done, 2 * s + h + 1)
                    y = ps[:, YB[(2 * s + h) % len(YB)], :]
                    nc.vector.scalar_tensor_tensor(t[:, cols], res[b][:, cols], ALPHA, y, ALU.mult,
                                                   ALU.add).then_inc(y_read, 1)
                    dve.wait_ge(y_read, 2 * s + h + 1)
                    stat = nc.vector.bn_stats(stats[:, b, h, :], t[:, cols])
                chain(stat)
                chain(nc.vector.bn_aggr(m[:, 0:2], stats[:, b, :, :]))
                nc.vector.tensor_scalar(var_eps, var, EPS, None, ALU.add).then_inc(var_ready, 1)
                if s == 0:
                    dve.wait_ge(lnp_loaded, 32)

                def center(i, end):
                    cols = slice(i * DM // 4, end * DM // 4)
                    return nc.vector.scalar_tensor_tensor(t[:, cols], t[:, cols], mean, ln_par[:, 0, cols],
                                                          ALU.subtract, ALU.mult)

                center(0, 2)
                if s + 4 < ST:
                    split_gated(EARLY + s + 4, s + 4, 0, PAIRS)
                dve.wait_ge(root_done, s + 1)
                chain(nc.vector.reciprocal(r, sd), lambda: center(2, 3))
                chain(nc.vector.tensor_scalar(c, var_eps, r, r, ALU.mult, ALU.mult), lambda: center(3, 4))
                chain(nc.vector.tensor_scalar(c, c, -0.5, 1.5, ALU.mult, ALU.add))
                chain(nc.vector.tensor_tensor(r, r, c, ALU.mult))
                for cols in STORES[s == ST - 1]:
                    nc.vector.scalar_tensor_tensor(res[b][:, cols], t[:, cols], r, ln_par[:, 1, cols], ALU.mult,
                                                   ALU.add).then_inc(normed, 1)

        @block.gpsimd
        def _(pool):
            def split_w(p, o, gates=None):
                if gates is not None:
                    pool.wait_ge(gated_done, gates)
                pool.wait_ge(w_loaded[o % 2], 16 * (2 * p + o // 2 + 1))
                if not (is_first(p) and o < 2):
                    pool.wait_ge(projected, 8 * p + 2 * o - 2)
                nc.gpsimd.tensor_tensor(w_hi[:, o % 2, :], w_raw[:, o % 2, :], ones[:, 0:1].broadcast_to([P, KT * P]),
                                        ALU.mult).then_inc(w_hi_done, 1)
                pool.wait_ge(w_hi_done, 4 * p + o)
                nc.gpsimd.tensor_tensor(w_lo[:, o % 2, :], w_raw[:, o % 2, :], w_hi[:, o % 2, :].bitcast(F32),
                                        ALU.subtract).then_inc(w_split, 1)

            def gate_o(p, unit, splits):
                head, half = UNITS[unit]
                pool.wait_ge(w_split, splits)
                if unit or not is_first(p):
                    pool.wait_ge(gated_done, 4 * p + unit)
                mine = slice(head * HEAD, (head + 1) * HEAD)
                cols = slice(half * HALF, (half + 1) * HALF)
                pool.wait_ge(o_summed, 4 * p + unit + 1)
                pool.wait_ge(bank_free[half], 4 * p + G_ + 1)
                nc.gpsimd.tensor_tensor(gated[mine, p, cols], osum[mine, half, :], silu[mine, cols],
                                        ALU.mult).then_inc(gated_done, 1)

            def split_wo(i):
                e = POOL_WO[i]
                pool.wait_ge(w_loaded[i % 2], 16 * (2 * PAIRS + i // 2 + 1))
                pool.wait_ge(x_used, e + 1)
                nc.gpsimd.tensor_tensor(wo_hi[:, e, :], w_raw[:, i % 2, :], ones[:, 0:1].broadcast_to([P, DM]),
                                        ALU.mult).then_inc(wo_hi_done, 1)
                pool.wait_ge(wo_hi_done, i + 1)
                nc.gpsimd.tensor_tensor(wo_lo[:, e, :], w_raw[:, i % 2, :], wo_hi[:, e, :].bitcast(F32),
                                        ALU.subtract).then_inc(wo_split, 1)

            def body(p, first=False, last=False):
                if first:
                    pool.wait_ge(w_split, V_)
                split_w(p, G_, None if first else 4 * p - 1)
                if not first:
                    gate_o(p - 1, 3, 4 * p + 3)
                if not last:
                    split_w(p + 1, K_, None if first else 4 * p)
                else:
                    pool.wait_ge(gated_done, 4 * p)
                    for i in range(len(POOL_WO)):
                        split_wo(i)
                    pool.wait_ge(wo_split, len(POOL_WO))
                gate_o(p, 0, 4 * p + (3 if last else 4))
                if not last:
                    split_w(p + 1, Q_, 4 * p + 1)
                gate_o(p, 1, 4 * p + (3 if last else 5))
                if not last:
                    split_w(p + 1, V_, 4 * p + 2)
                gate_o(p, 2, 4 * p + (3 if last else 6))

            nc.gpsimd.memset(ones[:, :], 1.0).then_inc(ones_set, 1)
            pool.wait_ge(ones_set, 1)
            pool.wait_ge(begin_loaded[Q_], 16)
            nc.gpsimd.tensor_tensor(w_hi[:, Q_, BEGIN], w_raw[:, Q_, BEGIN], ones[:, 0:1].broadcast_to([P, 2 * P]),
                                    ALU.mult).then_inc(q0_hi_done, 1)
            pool.wait_ge(q0_hi_done, 1)
            nc.gpsimd.tensor_tensor(w_lo[:, Q_, BEGIN], w_raw[:, Q_, BEGIN], w_hi[:, Q_, BEGIN].bitcast(F32),
                                    ALU.subtract).then_inc(q0_split, 1)
            pool.wait_ge(w_loaded[Q_], 16)
            nc.gpsimd.tensor_tensor(w_hi[:, Q_, REST], w_raw[:, Q_, REST],
                                    ones[:, 0:1].broadcast_to([P, (KT - 2) * P]), ALU.mult).then_inc(w_hi_done, 1)
            pool.wait_ge(w_hi_done, 1)
            nc.gpsimd.tensor_tensor(w_lo[:, Q_, REST], w_raw[:, Q_, REST], w_hi[:, Q_, REST].bitcast(F32),
                                    ALU.subtract).then_inc(w_split, 1)
            body(0, first=True)
            with pool.Fori(1, PAIRS - 1) as p:
                body(p)
            body(PAIRS - 1, last=True)

            gate_o(PAIRS - 1, 3, 4 * PAIRS - 1)


def kernel(x, w_in, w_out, ln_g, ln_b, rel_table):
    import concourse.bacc as bacc
    import ml_dtypes
    import numpy as np
    from concourse.bass_utils import run_bass_kernel_spmd

    x, w_in, w_out = np.asarray(x), np.asarray(w_in), np.asarray(w_out)
    rows = x[0, ::-1]
    w = w_in[0].reshape(KT, P, 4, PAIRS, P)[:, :, [1, 0, 2, 3]].transpose(3, 2, 1, 0, 4)
    one = np.eye(P, dtype=np.float32)
    arrays = {
        "xT": rows.T.reshape(KT, P, SEQ),
        "x_rows": rows.reshape(ST, P, DM),
        "w_in": w.reshape(PAIRS, 4, P, KT * P),
        "w_out": w_out[0].reshape(PAIRS, P, DM),
        "ln_g": np.asarray(ln_g),
        "ln_b": np.asarray(ln_b),
        "consts_f": one,
        "consts_b": np.eye(P, SEQ, 1).astype(ml_dtypes.bfloat16),
    }
    arrays = {f"in_{n}": np.ascontiguousarray(a) for n, a in arrays.items()}
    nc = bacc.Bacc("TRN2", target_bir_lowering=False, num_devices=1, dynamic_dma_scratch_size=4096)
    args = [nc.dram_tensor(n, a.shape, mybir.dt.from_np(a.dtype), kind="ExternalInput").ap()
            for n, a in arrays.items()]
    args.append(nc.dram_tensor("out_y", (ST, P, DM), F32, kind="ExternalOutput").ap())
    stick_breaking_layer(nc, *args)
    r = run_bass_kernel_spmd(nc, [arrays], core_ids=[0])
    y = np.asarray(r.results[0]["out_y"])
    return y.reshape(1, SEQ, DM)[:, ::-1]
```
